# Optimizing a Trainium2 kernel written in Bass

```python
import math
import jax, jax.numpy as jnp
from jax import lax
import numpy as np

D_MODEL = 1024
BATCH = 1
SEQ = 512
DEPTH = 2

CTX_LEN = 256
GRID_W = 64
N_MIXERS = 3
EPS = 1e-6
ROPE_THETA = 10000.0

GLA_HEADS = 4
GLA_DK = D_MODEL // 2 // GLA_HEADS
GLA_DV = D_MODEL // GLA_HEADS
GLA_GATE_RANK = 16
GLA_TAU = 16.0
GLA_CHUNK = 64

DIFF_HD = 64
DIFF_HEADS = D_MODEL // (2 * DIFF_HD)
DIFF_QBLOCK = 128

SSD_DINNER = 2 * D_MODEL
SSD_HEADDIM = 64
SSD_HEADS = SSD_DINNER // SSD_HEADDIM
SSD_STATE = 128
SSD_GROUPS = 4
SSD_CONV = 5
SSD_CHUNK = 128

PEER_KEYS = 128
PEER_EXPERTS = PEER_KEYS * PEER_KEYS
PEER_HEADS = 8
PEER_DKEY = 256
PEER_TOPK = 16
PEER_CHUNK = 128

kernel_name = "hybrid_gla_diffattn_ssd_peer_dit"

def rmsnorm(x, g):
    xf = x.astype(jnp.float32)
    xf = xf * lax.rsqrt(jnp.mean(jnp.square(xf), axis=-1, keepdims=True) + EPS)
    return (xf * g.astype(jnp.float32)).astype(x.dtype)

def modulate(h, shift, scale):
    return h * (1 + scale) + shift

def split_cols(t, widths):
    out, start = [], 0
    for w in widths:
        out.append(t[..., start:start + w])
        start += w
    return out

def flip(t):
    return jnp.flip(t, axis=1)

def lambda_init(layer_idx):
    return 0.8 - 0.6 * math.exp(-0.3 * layer_idx)

def axial_rope(rows):
    row = jnp.repeat(jnp.arange(rows), GRID_W).astype(jnp.float32)
    col = jnp.tile(jnp.arange(GRID_W), rows).astype(jnp.float32)
    n_freq = DIFF_HD // 4
    freqs = ROPE_THETA ** (-jnp.arange(n_freq, dtype=jnp.float32) / n_freq)
    ang = jnp.concatenate([row[:, None] * freqs, col[:, None] * freqs], axis=-1)
    return jnp.cos(ang), jnp.sin(ang)

def apply_rope(t, cos, sin):
    half = t.shape[-1] // 2
    cs, sn = cos[None, :, None, None, :], sin[None, :, None, None, :]
    t1, t2 = t[..., :half], t[..., half:]
    return jnp.concatenate([t1 * cs - t2 * sn, t1 * sn + t2 * cs], axis=-1).astype(t.dtype)

def gla_chunk_scan(q, k, v, log_a, s0):
    Bn, L, H, DK = q.shape
    DV = v.shape[-1]
    nc = L // GLA_CHUNK

    def to_chunks(t):
        return jnp.moveaxis(t.astype(jnp.float32).reshape(Bn, nc, GLA_CHUNK, H, t.shape[-1]), 1, 0)

    mask = jnp.tril(jnp.ones((GLA_CHUNK, GLA_CHUNK), bool))[None, :, :, None, None]

    def step(s, inp):
        qc, kc, vc, ac = inp
        b = jnp.cumsum(ac, axis=1)
        seg = b[:, :, None] - b[:, None, :]
        decay = jnp.exp(jnp.where(mask, seg, -jnp.inf))
        scores = jnp.sum(qc[:, :, None] * kc[:, None, :] * decay, axis=-1)
        o = jnp.einsum('bijh,bjhv->bihv', scores, vc)
        o = o + jnp.einsum('bihd,bhdv->bihv', qc * jnp.exp(b), s)
        b_last = b[:, -1]
        k_dec = kc * jnp.exp(b_last[:, None] - b)
        s = jnp.exp(b_last)[..., None] * s + jnp.einsum('bjhd,bjhv->bhdv', k_dec, vc)
        return s, o

    s_fin, o = lax.scan(step, s0, (to_chunks(q), to_chunks(k), to_chunks(v), to_chunks(log_a)))
    return jnp.moveaxis(o, 0, 1).reshape(Bn, L, H, DV), s_fin

def gla_project(h, w_in, w_alpha, b_alpha):
    Bn, L, _ = h.shape
    hk, hv = GLA_HEADS * GLA_DK, GLA_HEADS * GLA_DV
    q, k, v, g, lo_f, lo_b = split_cols(h @ w_in, (hk, hk, hv, hv, GLA_GATE_RANK, GLA_GATE_RANK))
    q = q.reshape(Bn, L, GLA_HEADS, GLA_DK) * (GLA_DK ** -0.5)
    k = k.reshape(Bn, L, GLA_HEADS, GLA_DK)
    v = v.reshape(Bn, L, GLA_HEADS, GLA_DV)

    def log_gate(lo, d):
        z = (lo @ w_alpha[d] + b_alpha[d]).astype(jnp.float32)
        return (jax.nn.log_sigmoid(z) / GLA_TAU).reshape(Bn, L, GLA_HEADS, GLA_DK)

    return q, k, v, g, log_gate(lo_f, 0), log_gate(lo_b, 1)

def gla_mixer(h_ctx, h_lat, w_in, w_alpha, b_alpha, norm_g, w_out, ctx_out):
    def scans(proj, s_f0, s_b0):
        q, k, v, g, la_f, la_b = proj
        o_f, s_f = gla_chunk_scan(q, k, v, la_f, s_f0)
        o_b, s_b = gla_chunk_scan(flip(q), flip(k), flip(v), flip(la_b), s_b0)
        return (o_f + flip(o_b)).astype(v.dtype), g, s_f, s_b

    def finish(o, g):
        o = rmsnorm(o, norm_g).reshape(g.shape) * jax.nn.silu(g)
        return o @ w_out

    s0 = jnp.zeros((h_ctx.shape[0], GLA_HEADS, GLA_DK, GLA_DV), jnp.float32)
    o_c, g_c, s_f, s_b = scans(gla_project(h_ctx, w_in, w_alpha, b_alpha), s0, s0)
    o_l, g_l, _, _ = scans(gla_project(h_lat, w_in, w_alpha, b_alpha), s_f, s_b)
    return (finish(o_c, g_c) if ctx_out else None), finish(o_l, g_l)

def diff_project(h, w_in):
    Bn, L, _ = h.shape
    wd = DIFF_HEADS * 2 * DIFF_HD
    q, k, v = split_cols(h @ w_in, (wd, wd, wd))
    return (q.reshape(Bn, L, DIFF_HEADS, 2, DIFF_HD), k.reshape(Bn, L, DIFF_HEADS, 2, DIFF_HD),
            v.reshape(Bn, L, DIFF_HEADS, 2 * DIFF_HD))

def diff_attend(q, k, v, lam):
    Bn, Lq = q.shape[:2]
    nb = Lq // DIFF_QBLOCK
    qb = jnp.moveaxis(q.reshape(Bn, nb, DIFF_QBLOCK, DIFF_HEADS, 2, DIFF_HD), 1, 0)

    def block(qi):
        s = jnp.einsum('bqhmd,bkhmd->bhmqk', qi, k).astype(jnp.float32) * (DIFF_HD ** -0.5)
        p = jax.nn.softmax(s, axis=-1)
        a = p[:, :, 0] - lam * p[:, :, 1]
        return jnp.einsum('bhqk,bkhv->bqhv', a.astype(v.dtype), v)

    o = lax.map(block, qb)
    return jnp.moveaxis(o, 0, 1).reshape(Bn, Lq, DIFF_HEADS, 2 * DIFF_HD)

def diff_mixer(h_ctx, h_lat, w_in, lam_vecs, norm_g, w_out, cos, sin, lam_init, ctx_out):
    lv = lam_vecs.astype(jnp.float32)
    lam = jnp.exp(jnp.sum(lv[0] * lv[1])) - jnp.exp(jnp.sum(lv[2] * lv[3])) + lam_init
    q_c, k_c, v_c = diff_project(h_ctx, w_in)
    q_l, k_l, v_l = diff_project(h_lat, w_in)
    q_l = apply_rope(q_l, cos, sin)
    k_l = apply_rope(k_l, cos, sin)

    def finish(o):
        o = rmsnorm(o, norm_g) * (1 - lam_init)
        return o.reshape(o.shape[0], o.shape[1], -1) @ w_out

    o_l = diff_attend(q_l, jnp.concatenate([k_c, k_l], axis=1), jnp.concatenate([v_c, v_l], axis=1), lam)
    o_c = finish(diff_attend(q_c, k_c, v_c, lam)) if ctx_out else None
    return o_c, finish(o_l)

def dwconv_centred(t, w, b):
    y = lax.conv_general_dilated(t, w[:, None, :].astype(t.dtype), window_strides=(1,),
                                 padding=((SSD_CONV // 2, SSD_CONV // 2),),
                                 dimension_numbers=('NWC', 'WIO', 'NWC'), feature_group_count=t.shape[-1])
    return y + b

def ssd_project(h, w_in, conv_w, conv_b, dt_bias):
    Bn, L, _ = h.shape
    gn = SSD_GROUPS * SSD_STATE
    z, xbc, dt = split_cols(h @ w_in, (SSD_DINNER, SSD_DINNER + 2 * gn, 2 * SSD_HEADS))
    xbc = jax.nn.silu(dwconv_centred(xbc, conv_w, conv_b))
    xs, bm, cm = split_cols(xbc, (SSD_DINNER, gn, gn))
    xs = xs.reshape(Bn, L, SSD_HEADS, SSD_HEADDIM)
    bm = bm.reshape(Bn, L, SSD_GROUPS, SSD_STATE)
    cm = cm.reshape(Bn, L, SSD_GROUPS, SSD_STATE)
    dt = jax.nn.softplus(dt.astype(jnp.float32).reshape(Bn, L, 2, SSD_HEADS) + dt_bias.astype(jnp.float32))
    return z, xs, bm, cm, dt

def ssd_chunk_scan(xs, dt, a, bm, cm, h0):
    Bn, L = xs.shape[:2]
    nc, Q, R = L // SSD_CHUNK, SSD_CHUNK, SSD_HEADS // SSD_GROUPS
    xg = xs.astype(jnp.float32).reshape(Bn, nc, Q, SSD_GROUPS, R, SSD_HEADDIM)
    dg = dt.reshape(Bn, nc, Q, SSD_GROUPS, R)
    bg = bm.astype(jnp.float32).reshape(Bn, nc, Q, SSD_GROUPS, SSD_STATE)
    cg = cm.astype(jnp.float32).reshape(Bn, nc, Q, SSD_GROUPS, SSD_STATE)
    ag = a.reshape(SSD_GROUPS, R)
    mask = jnp.tril(jnp.ones((Q, Q), bool))[None, :, :, None, None]

    def step(h, inp):
        xc, dc, bc, cc = inp
        acum = jnp.cumsum(dc * ag, axis=1)
        seg = acum[:, :, None] - acum[:, None, :]
        lmat = jnp.exp(jnp.where(mask, seg, -jnp.inf))
        cb = jnp.einsum('bign,bjgn->bijg', cc, bc)
        w = cb[..., None] * lmat * dc[:, None]
        y = jnp.einsum('bijgr,bjgrp->bigrp', w, xc)
        y = y + jnp.einsum('bign,bgrpn->bigrp', cc, h) * jnp.exp(acum)[..., None]
        a_last = acum[:, -1]
        wt = jnp.exp(a_last[:, None] - acum) * dc
        h = jnp.exp(a_last)[..., None, None] * h + jnp.einsum('bjgr,bjgrp,bjgn->bgrpn', wt, xc, bc)
        return h, y

    chunks = tuple(jnp.moveaxis(t, 1, 0) for t in (xg, dg, bg, cg))
    h_fin, y = lax.scan(step, h0, chunks)
    return jnp.moveaxis(y, 0, 1).reshape(Bn, L, SSD_HEADS, SSD_HEADDIM), h_fin

def ssd_mixer(h_ctx, h_lat, w_in, conv_w, conv_b, dt_bias, a_log, d_skip, norm_g, w_out, ctx_out):
    a = -jnp.exp(a_log.astype(jnp.float32))
    gsz = SSD_DINNER // SSD_GROUPS

    def scans(h, hf0, hb0):
        z, xs, bm, cm, dt = ssd_project(h, w_in, conv_w, conv_b, dt_bias)
        y_f, hf = ssd_chunk_scan(xs, dt[:, :, 0], a[0], bm, cm, hf0)
        y_b, hb = ssd_chunk_scan(flip(xs), flip(dt[:, :, 1]), a[1], flip(bm), flip(cm), hb0)
        y = y_f + flip(y_b) + d_skip.astype(jnp.float32)[:, None] * xs.astype(jnp.float32)
        return y, z, hf, hb

    def finish(y, z):
        Bn, L = z.shape[:2]
        y = y.reshape(Bn, L, SSD_DINNER).astype(z.dtype) * jax.nn.silu(z)
        y = rmsnorm(y.reshape(Bn, L, SSD_GROUPS, gsz), norm_g.reshape(SSD_GROUPS, gsz)).reshape(Bn, L, SSD_DINNER)
        return y @ w_out

    h0 = jnp.zeros((h_ctx.shape[0], SSD_GROUPS, SSD_HEADS // SSD_GROUPS, SSD_HEADDIM, SSD_STATE), jnp.float32)
    y_c, z_c, hf, hb = scans(h_ctx, h0, h0)
    y_l, z_l, _, _ = scans(h_lat, hf, hb)
    return (finish(y_c, z_c) if ctx_out else None), finish(y_l, z_l)

def peer_ffn(h, wq, subkeys, u, v):
    Bn, L, D = h.shape
    hc = h.reshape(Bn * L // PEER_CHUNK, PEER_CHUNK, D)

    def block(xc):
        C = xc.shape[0]
        q = (xc @ wq).reshape(C, PEER_HEADS, 2, PEER_DKEY // 2)
        s = jnp.einsum('chzd,zkd->chzk', q, subkeys).astype(jnp.float32)
        top_s, top_i = lax.top_k(s, PEER_TOPK)
        cand_s = (top_s[:, :, 0, :, None] + top_s[:, :, 1, None, :]).reshape(C, PEER_HEADS, -1)
        cand_i = (top_i[:, :, 0, :, None] * PEER_KEYS + top_i[:, :, 1, None, :]).reshape(C, PEER_HEADS, -1)
        best_s, best_j = lax.top_k(cand_s, PEER_TOPK)
        idx = jnp.take_along_axis(cand_i, best_j, axis=-1)
        g = jax.nn.softmax(best_s, axis=-1)
        ue = jnp.take(u, idx, axis=0)
        ve = jnp.take(v, idx, axis=0)
        act = jax.nn.gelu(jnp.einsum('cd,chkd->chk', xc, ue).astype(jnp.float32), approximate=False)
        return jnp.einsum('chk,chkd->cd', (g * act).astype(ve.dtype), ve)

    return lax.map(block, hc).reshape(Bn, L, D)

def setup_inputs(seed: int = 0) -> dict:
    key = jax.random.key(seed)
    ks = iter(jax.random.split(key, 40))

    def nrm(shape, scale):
        return jax.random.normal(next(ks), shape, jnp.float32) * scale

    def gain(shape):
        return 1.0 + nrm(shape, 0.02)

    n_a = len(range(0, DEPTH, N_MIXERS))
    n_b = len(range(1, DEPTH, N_MIXERS))
    n_c = len(range(2, DEPTH, N_MIXERS))
    D = D_MODEL
    gla_in = 2 * GLA_HEADS * GLA_DK + 2 * GLA_HEADS * GLA_DV + 2 * GLA_GATE_RANK
    diff_in = 3 * DIFF_HEADS * 2 * DIFF_HD
    conv_ch = SSD_DINNER + 2 * SSD_GROUPS * SSD_STATE
    ssd_in = SSD_DINNER + conv_ch + 2 * SSD_HEADS
    dt0 = jnp.exp(jax.random.uniform(next(ks), (n_c, 2, SSD_HEADS), jnp.float32,
                                     minval=math.log(1e-3), maxval=math.log(1e-1)))
    a0 = jax.random.uniform(next(ks), (n_c, 2, SSD_HEADS), jnp.float32, minval=1.0, maxval=16.0)
    return {
        "x": nrm((BATCH, SEQ, D), 1.0),
        "c": nrm((BATCH, D), 1.0),
        "ctx": nrm((BATCH, CTX_LEN, D), 1.0),
        "c_ctx": nrm((D,), 1.0),
        "norm1_g": gain((DEPTH, D)),
        "norm2_g": gain((DEPTH, D)),
        "w_mod": nrm((DEPTH, D, 6 * D), 0.5 * D ** -0.5),
        "b_mod": nrm((DEPTH, 6 * D), 0.02),
        "peer_wq": nrm((DEPTH, D, PEER_HEADS * PEER_DKEY), D ** -0.5),
        "peer_subkeys": nrm((DEPTH, 2, PEER_KEYS, PEER_DKEY // 2), (PEER_DKEY // 2) ** -0.5),
        "peer_u": nrm((DEPTH, PEER_EXPERTS, D), D ** -0.5),
        "peer_v": nrm((DEPTH, PEER_EXPERTS, D), (PEER_HEADS * PEER_TOPK) ** -0.5),
        "gla_w_in": nrm((n_a, D, gla_in), D ** -0.5),
        "gla_w_alpha": nrm((n_a, 2, GLA_GATE_RANK, GLA_HEADS * GLA_DK), GLA_GATE_RANK ** -0.5),
        "gla_b_alpha": nrm((n_a, 2, GLA_HEADS * GLA_DK), 0.5),
        "gla_norm_g": gain((n_a, GLA_DV)),
        "gla_w_out": nrm((n_a, GLA_HEADS * GLA_DV, D), (GLA_HEADS * GLA_DV) ** -0.5),
        "diff_w_in": nrm((n_b, D, diff_in), D ** -0.5),
        "diff_lambda": nrm((n_b, 4, DIFF_HD), 0.1),
        "diff_norm_g": gain((n_b, 2 * DIFF_HD)),
        "diff_w_out": nrm((n_b, DIFF_HEADS * 2 * DIFF_HD, D), (DIFF_HEADS * 2 * DIFF_HD) ** -0.5),
        "ssd_w_in": nrm((n_c, D, ssd_in), D ** -0.5),
        "ssd_conv_w": nrm((n_c, SSD_CONV, conv_ch), SSD_CONV ** -0.5),
        "ssd_conv_b": nrm((n_c, conv_ch), 0.02),
        "ssd_dt_bias": dt0 + jnp.log(-jnp.expm1(-dt0)),
        "ssd_a_log": jnp.log(a0),
        "ssd_d": gain((n_c, SSD_HEADS)),
        "ssd_norm_g": gain((n_c, SSD_DINNER)),
        "ssd_w_out": nrm((n_c, SSD_DINNER, D), SSD_DINNER ** -0.5),
        "final_g": gain((D,)),
    }

def reference(x, c, ctx, c_ctx, norm1_g, norm2_g, w_mod, b_mod,
              peer_wq, peer_subkeys, peer_u, peer_v,
              gla_w_in, gla_w_alpha, gla_b_alpha, gla_norm_g, gla_w_out,
              diff_w_in, diff_lambda, diff_norm_g, diff_w_out,
              ssd_w_in, ssd_conv_w, ssd_conv_b, ssd_dt_bias, ssd_a_log, ssd_d, ssd_norm_g, ssd_w_out,
              final_g):
    n_ctx = ctx.shape[1]
    rows = x.shape[1] // GRID_W
    cos, sin = axial_rope(rows)
    cond_lat = jax.nn.silu(c)[:, None, :]
    cond_ctx = jax.nn.silu(c_ctx)[None, None, :]
    h_lat, h_ctx = x, ctx
    for i in range(DEPTH):
        kind, j = i % N_MIXERS, i // N_MIXERS
        last = i == DEPTH - 1
        mod_l = split_cols(cond_lat @ w_mod[i] + b_mod[i], (D_MODEL,) * 6)
        mod_c = split_cols(cond_ctx @ w_mod[i] + b_mod[i], (D_MODEL,) * 6)
        a_lat = modulate(rmsnorm(h_lat, norm1_g[i]), mod_l[0], mod_l[1])
        a_ctx = modulate(rmsnorm(h_ctx, norm1_g[i]), mod_c[0], mod_c[1])
        if kind == 0:
            o_ctx, o_lat = gla_mixer(a_ctx, a_lat, gla_w_in[j], gla_w_alpha[j], gla_b_alpha[j],
                                     gla_norm_g[j], gla_w_out[j], not last)
        elif kind == 1:
            o_ctx, o_lat = diff_mixer(a_ctx, a_lat, diff_w_in[j], diff_lambda[j], diff_norm_g[j],
                                      diff_w_out[j], cos, sin, lambda_init(i), not last)
        else:
            o_ctx, o_lat = ssd_mixer(a_ctx, a_lat, ssd_w_in[j], ssd_conv_w[j], ssd_conv_b[j], ssd_dt_bias[j],
                                     ssd_a_log[j], ssd_d[j], ssd_norm_g[j], ssd_w_out[j], not last)
        h_lat = h_lat + mod_l[2] * o_lat
        f_lat = modulate(rmsnorm(h_lat, norm2_g[i]), mod_l[3], mod_l[4])
        if last:
            h_lat = h_lat + mod_l[5] * peer_ffn(f_lat, peer_wq[i], peer_subkeys[i], peer_u[i], peer_v[i])
        else:
            h_ctx = h_ctx + mod_c[2] * o_ctx
            f_ctx = modulate(rmsnorm(h_ctx, norm2_g[i]), mod_c[3], mod_c[4])
            f = peer_ffn(jnp.concatenate([f_ctx, f_lat], axis=1), peer_wq[i], peer_subkeys[i], peer_u[i], peer_v[i])
            h_ctx = h_ctx + mod_c[5] * f[:, :n_ctx]
            h_lat = h_lat + mod_l[5] * f[:, n_ctx:]
    return rmsnorm(h_lat, final_g)


_drawn_inputs = setup_inputs


def setup_inputs(seed=0):
    import zlib

    import numpy as np

    out = dict(_drawn_inputs(seed))
    spreads = {}
    factors = {'norm1_g': 6.771,
     'norm2_g': 8.0,
     'peer_wq': 3.077,
     'peer_subkeys': 3.074,
     'peer_u': 3.411,
     'peer_v': 3.052,
     'gla_norm_g': 8.0,
     'diff_lambda': 2.838,
     'diff_norm_g': 48.602,
     'final_g': 8.971}
    for name, (base, spread) in spreads.items():
        noise = np.random.default_rng([zlib.crc32(name.encode()), seed]).standard_normal(out[name].shape)
        drawn = base * np.exp(spread * noise) if base else spread * noise
        out[name] = __import__('jax').numpy.asarray(drawn.astype(out[name].dtype))
    for name, factor in factors.items():
        out[name] = (out[name] * factor).astype(out[name].dtype)
    return out
```

```python
import math
from contextlib import ExitStack

import numpy as np
import concourse.bass as bass
from concourse import mybir
from concourse.alu_op_type import AluOpType as ALU

F32 = mybir.dt.float32
F32R = mybir.dt.float32r
U32 = mybir.dt.uint32
ACT = mybir.ActivationFunctionType
AX = mybir.AxisListType
ds = bass.ds

P = 128
D = 1024
C = D // P
NCTX = 256
NLAT = 512
T = NCTX + NLAT
CTX, LAT = (0, NCTX, 0), (NCTX, NLAT, 1)
DEPTH = 2
EPS = 1e-6

GLA_HEADS = 4
GLA_DV = D // GLA_HEADS
GLA_RANK = 16
GLA_TAU = 16.0
LEVELS = 7
TO_START, TO_END = LEVELS, LEVELS + 1
CHUNKS = T // P
CTX_CHUNKS = NCTX // P
FORWARD = list(range(CHUNKS))
BACKWARD = list(range(CTX_CHUNKS))[::-1] + list(range(CTX_CHUNKS, CHUNKS))[::-1]
NMASK = 2 * LEVELS + 1

HD = 64
DIFF_HEADS = D // (2 * HD)
GRID_W = 64
LAMBDA_INIT = 0.8 - 0.6 * math.exp(-0.3 * 1)

HEADS = 8
KEYS = 128
TOPK = 16
PAIRS = HEADS * TOPK
TG = 64
JB = 2
QUAD = 4
MIXER_ARENA = 38100
PEER_ARENA = MIXER_ARENA - 2 * C * T
PART_ARENA = 14336
LOWEST = -3.0e38



def gla_range_sums():
    m = np.zeros((2, P, LEVELS + 2, P), np.float32)
    for t in range(P):
        for level in range(LEVELS):
            b = 1 << level
            mid = t // (2 * b) * (2 * b) + b
            if t >= mid:
                m[0, mid:t + 1, level, t] = 1
                m[1, mid:t, level, t] = 1
            else:
                m[0, t + 1:mid, level, t] = 1
                m[1, t:mid, level, t] = 1
        m[0, :t + 1, TO_START, t] = 1
        m[0, t + 1:, TO_END, t] = 1
        m[1, t:, TO_START, t] = 1
        m[1, :t, TO_END, t] = 1
    return m.reshape(2, P, -1)


def gla_masks():
    m = np.zeros((P, NMASK, P), np.float32)
    for j in range(P):
        for i in range(P):
            if i == j:
                m[j, NMASK - 1, i] = 2
                continue
            level = (i ^ j).bit_length() - 1
            m[j, level if i > j else LEVELS + level, i] = 1
    return m.reshape(P, -1)


def rope_tables():
    n = HD // 4
    freqs = np.float32(10000.0) ** (-np.arange(n, dtype=np.float32) / np.float32(n))
    rows = NLAT // GRID_W
    row = np.repeat(np.arange(rows), GRID_W).astype(np.float32)
    col = np.tile(np.arange(GRID_W), rows).astype(np.float32)
    angle = np.concatenate([row[:, None] * freqs, col[:, None] * freqs], -1).astype(np.float32)
    angle = np.tile(angle.T, (P // (HD // 2), 1)).astype(np.float64)
    swap = np.zeros((P, P), np.float32)
    for p in range(P):
        if p % HD < HD // 2:
            swap[p + HD // 2, p] = -1
        else:
            swap[p - HD // 2, p] = 1
    return np.cos(angle).astype(np.float32), np.sin(angle).astype(np.float32), swap


class Names:
    pass


class Chain:

    def __init__(self, sem):
        self.sem, self.base, self.n, self.turn = sem, 0, 0, None

    def loop(self, turn, per):
        self.turn, self.per = turn, per

    def inc(self, ins):
        ins.then_inc(self.sem, 1)
        self.n += 1

    def wait(self, engine):
        at = self.base + self.n
        engine.wait_ge(self.sem, at if self.turn is None else self.turn * self.per + at)

    def done(self, engine, ins):
        self.inc(ins)
        self.wait(engine)

    def end(self, turns):
        assert self.n == self.per, self.n
        self.base += turns * self.per
        self.n, self.turn = 0, None


def build(nc, a, out):
    ctx = ExitStack()
    with ctx:
        def sem(name):
            return ctx.enter_context(nc.semaphore(name))

        def sb(name, width, dt=F32):
            return ctx.enter_context(nc.sbuf_tensor(name, [P, width], dt))

        B = Names()
        B.a, B.out = a, out
        held, B.again = {}, []

        def stage_sem(name):
            if name in held:
                B.again.append(held[name])
            else:
                held[name] = sem(name)
            return held[name]

        B.sem = stage_sem
        B.ps = ctx.enter_context(nc.psum_tensor("ps", [P, 8, 512], F32))
        B.h = sb("hidden", C * T)[:, :].rearrange("p (c t) -> p c t", c=C)
        B.x = sb("mixer_in", C * T)[:, :].rearrange("p (c t) -> p c t", c=C)
        B.mod = sb("modulation", DEPTH * 6 * C * 2)[:, :].rearrange("p (l k c s) -> p l k c s", l=DEPTH, k=6, s=2)
        small = sb("small", 4 * C + C + 5 * 2)
        B.gains = small[:, 0:5 * C].rearrange("p (n c) -> p n c", n=5)
        B.ident = sb("identity", P)
        B.ones = sb("ones", P)
        B.chosen = [sb(f"chosen{n}", T // P * PAIRS)[:, :] for n in range(3)]
        with nc.sbuf_tensor("mixer_arena", [P, MIXER_ARENA], F32) as whole:
            B.mixer_arena = whole
        B.xr = sb("ffn_in_parts", 2 * C * T, F32R)[:, :].rearrange("p (s c t) -> p s c t", s=2, c=C)
        with nc.sbuf_tensor("gate_arena", [P, PEER_ARENA], F32) as whole:
            B.gate_arena = whole
        B.part_arena = sb("part_arena", PART_ARENA, F32R)
        B.peer_arena = sb("peer_arena", PEER_ARENA - PART_ARENA)
        B.g_dram = nc.dram_tensor("gates", (T // TG, P, KEYS * TG), F32, kind="Internal").ap()

        start_in = sem("start_in")
        plan = [(modulation,)]
        for layer, segs in ((0, (CTX, LAT)), (1, (LAT,))):
            plan += [(norm, layer, B.gains[:, layer], 0, 1, (CTX, LAT)),
                     (gla,) if layer == 0 else (attention,),
                     (project_out, a["gla_w_out"] if layer == 0 else a["diff_w_out"], segs[0][0], layer, segs),
                     (norm, layer, B.gains[:, 2 + layer], 3, 4, segs, True),
                     (product_keys, layer, segs),
                     (gates, segs),
                     (experts, layer, segs)]
        plan += [(norm, 1, B.gains[:, 4], None, None, (LAT,))]
        stages = []
        for make, *args in plan:
            B.again = []
            stage = make(B, *args)
            stage["again"] = B.again
            stages.append(stage)
        out_written = sem("out_written")
        stage_done, cleared = sem("stage_done"), sem("cleared")

        def run(engine, which):
            def meet():
                engine.drain().then_inc(stage_done, 1)
                meetings.append(1)
                engine.wait_ge(stage_done, 5 * len(meetings))

            meetings, clears = [], []
            for stage in stages:
                if which == "sync":
                    for s in stage["again"]:
                        engine.sem_clear(s).then_inc(cleared, 1)
                clears.extend(stage["again"])
                if stage["again"]:
                    engine.wait_ge(cleared, len(clears))
                    engine.drain()
                if which in stage:
                    stage[which](engine)
                meet()

        block = ctx.enter_context(nc.Block())

        @block.sync
        def _(sp):
            sp.dma_start(B.h[:, :, :], a["hidden"]).then_inc(start_in, 16)
            sp.dma_start(small[:, 0:5 * C], a["gains"]).then_inc(start_in, 16)
            sp.dma_start(B.ident[:, :], a["ident"]).then_inc(start_in, 16)
            sp.wait_ge(start_in, 48)
            run(sp, "sync")
            sp.dma_start(out, B.x[:, :, NCTX:]).then_inc(out_written, 16)
            sp.wait_ge(out_written, 16)

        @block.tensor
        def _(pe):
            run(pe, "tensor")

        @block.vector
        def _(dve):
            dve.memset(B.ones[:, :], 1.0)
            run(dve, "vector")

        @block.scalar
        def _(act):
            run(act, "scalar")

        @block.gpsimd
        def _(pool):
            run(pool, "gpsimd")


class Arena:

    def __init__(self, ap):
        self.ap, self.at = ap, 0

    def take(self, width, dt=None):
        v = self.ap[:, self.at:self.at + width]
        self.at += width
        return v if dt is None else v.bitcast(dt)



def modulation(B):
    M = 4
    blocks = DEPTH * 6 * C // M
    ar = Arena(B.mixer_arena)
    w = [ar.take(M * C * P).rearrange("p (m c n) -> p m c n", m=M, c=C) for _ in range(2)]
    raw = ar.take(C * 2).rearrange("p (c s) -> p c s", s=2)
    cond = ar.take(C * 2).rearrange("p (c s) -> p c s", s=2)
    bias = ar.take(blocks * M)
    mod = B.mod.rearrange("p l k c s -> p (l k c) s")
    cond_in, w_in = B.sem("cond_in"), [B.sem("mod_w_in0"), B.sem("mod_w_in1")]
    cond_ready, w_used, summed, added = (B.sem("mod_" + n) for n in ("cond", "w_used", "summed", "added"))

    def sync(sp):
        sp.dma_start(raw, B.a["cond"]).then_inc(cond_in, 16)
        sp.dma_start(bias, B.a["b_mod"]).then_inc(cond_in, 16)
        with sp.Fori(0, blocks // 2) as i:
            for s in range(2):
                sp.wait_ge(w_used, 2 * i + s + 1)
                sp.dma_start(w[s], B.a["w_mod"][ds(2 * i + s, 1)].squeeze(0)).then_inc(w_in[s], 16)

    def tensor(pe):
        pe.sem_inc(w_used, 2)
        pe.wait_ge(cond_ready, 1)
        with pe.Fori(0, blocks // 2) as i:
            for s in range(2):
                pe.wait_ge(w_in[s], 16 * i + 16)
                pe.wait_ge(added, 2 * i + s + 1)
                for m in range(M):
                    for c in range(C):
                        mm = pe.matmul(B.ps[:, s, 2 * m:2 * m + 2], w[s][:, m, c, :], cond[:, c, :],
                                       start=c == 0, stop=c == C - 1)
                mm.then_inc(summed, 1)
                pe.wait_ge(summed, 2 * i + s + 1)
                pe.sem_inc(w_used, 1)

    def scalar(act):
        act.wait_ge(cond_in, 32)
        act.activation(cond, raw, ACT.Silu).then_inc(cond_ready, 1)

    def vector(dve):
        dve.sem_inc(added, 2)
        dve.wait_ge(cond_in, 32)
        with dve.Fori(0, blocks // 2) as i:
            for s in range(2):
                dve.wait_ge(summed, 2 * i + s + 1)
                dve.tensor_tensor(mod[:, ds((2 * i + s) * M, M), :],
                                  B.ps[:, s, 0:2 * M].rearrange("p (m s) -> p m s", s=2),
                                  bias[:, ds((2 * i + s) * M, M)].unsqueeze(2).to_broadcast([P, M, 2]),
                                  ALU.add).then_inc(added, 1)

    return {"sync": sync, "tensor": tensor, "scalar": scalar, "vector": vector}



def norm(B, layer, gain, shift, scale, segs, split=False):
    dst = B.x
    ar = Arena(B.peer_arena if split else B.mixer_arena)
    t0, n = segs[0][0], sum(s[1] for s in segs)
    sq = [ar.take(T) for _ in range(2)]
    ms, r, tmp = ar.take(T), ar.take(T), ar.take(T)
    factor = ar.take(C * 2).rearrange("p (c s) -> p c s", s=2)
    used, squared, root, chain_s, scaled, shifted, high = (
        B.sem(f"norm_{x}") for x in ("used", "squared", "root", "chain", "scaled", "shifted", "high"))

    def scalar(act):
        for c in range(C):
            act.wait_ge(used, c + 1)
            act.activation(sq[c % 2][:, t0:t0 + n], B.h[:, c, t0:t0 + n], ACT.Square).then_inc(squared, 1)
        act.wait_ge(chain_s, 2 if len(segs) == 1 else 3)
        act.activation(r[:, t0:t0 + n], ms[:, t0:t0 + n], ACT.Sqrt).then_inc(root, 1)
        if shift is not None:
            for c in range(C):
                act.wait_ge(scaled, c + 1)
                for (s0, m, which) in segs:
                    ins = act.activation(dst[:, c, s0:s0 + m], dst[:, c, s0:s0 + m], ACT.Identity,
                                         bias=B.mod[:, layer, shift, c, which:which + 1])
                ins.then_inc(shifted, 1)
                if split:
                    act.wait_ge(shifted, c + 1)
                    act.copy(B.xr[:, 0, c, t0:t0 + n], dst[:, c, t0:t0 + n]).then_inc(high, 1)

    def tensor(pe):
        pe.sem_inc(used, 2)
        for c in range(C):
            pe.wait_ge(squared, c + 1)
            for (s0, m, which) in segs:
                mm = pe.matmul(B.ps[:, which, 0:m], B.ones[:, :], sq[c % 2][:, s0:s0 + m],
                               start=c == 0, stop=c == C - 1)
            mm.then_inc(used, 1)

    def vector(dve):
        chain = Chain(chain_s)
        if shift is not None:
            chain.inc(dve.scalar_tensor_tensor(out=factor, in0=B.mod[:, layer, scale], scalar=1.0,
                                               in1=gain.unsqueeze(2).to_broadcast([P, C, 2]),
                                               op0=ALU.add, op1=ALU.mult))
        else:
            chain.inc(dve.tensor_copy(factor, gain.unsqueeze(2).to_broadcast([P, C, 2])))
        dve.wait_ge(used, C + 2)
        for (s0, m, which) in segs:
            chain.inc(dve.tensor_scalar(ms[:, s0:s0 + m], B.ps[:, which, 0:m], 1.0 / D, EPS, ALU.mult, ALU.add))
        dve.wait_ge(root, 1)
        refined_reciprocal(dve, chain, r[:, t0:t0 + n], ms[:, t0:t0 + n], tmp[:, t0:t0 + n])
        for c in range(C):
            for (s0, m, which) in segs:
                ins = dve.scalar_tensor_tensor(out=dst[:, c, s0:s0 + m], in0=B.h[:, c, s0:s0 + m],
                                               scalar=factor[:, c, which:which + 1], in1=r[:, s0:s0 + m],
                                               op0=ALU.mult, op1=ALU.mult)
            ins.then_inc(scaled, 1)
        if split:
            for c in range(C):
                dve.wait_ge(high, c + 1)
                dve.tensor_tensor(B.xr[:, 1, c, t0:t0 + n], dst[:, c, t0:t0 + n],
                                  B.xr[:, 0, c, t0:t0 + n].bitcast(F32), ALU.subtract)

    def refined_reciprocal(dve, chain, r, ms, tmp):
        chain.wait(dve)
        chain.done(dve, dve.reciprocal(r, r))
        chain.done(dve, dve.tensor_tensor(tmp, r, r, ALU.mult))
        chain.done(dve, dve.tensor_tensor(tmp, tmp, ms, ALU.mult))
        chain.done(dve, dve.tensor_scalar(tmp, tmp, -0.5, 1.5, ALU.mult, ALU.add))
        chain.done(dve, dve.tensor_tensor(r, r, tmp, ALU.mult))

    return {"scalar": scalar, "tensor": tensor, "vector": vector}



def gla(B):
    H, DV2 = GLA_HEADS, GLA_DV // P
    ar = Arena(B.mixer_arena)
    oT = ar.take(C * T).rearrange("p (c t) -> p c t", c=C)
    wqkg = ar.take(C * 512).rearrange("p (c n) -> p c n", c=C)
    wv = ar.take(C * GLA_DV).rearrange("p (c n) -> p c n", c=C)
    wlo = ar.take(C * 2 * GLA_RANK).rearrange("p (c n) -> p c n", c=C)
    lo = ar.take(2 * T).rearrange("p (d t) -> p d t", d=2)
    walpha = ar.take(2 * 512).rearrange("p (d n) -> p d n", d=2)
    sums = [ar.take((LEVELS + 2) * P) for _ in range(2)]
    masks = ar.take(NMASK * P)
    q, k = ar.take(T), ar.take(T)
    g = ar.take(DV2 * T).rearrange("p (v t) -> p v t", v=DV2)
    v = ar.take(CHUNKS * GLA_DV).rearrange("p (n v) -> p n v", n=CHUNKS)
    la = ar.take(2 * CHUNKS * P)
    soft = ar.take(2 * CHUNKS * P)
    dec_f, dec_b = ar.take((LEVELS + 2) * P), ar.take(LEVELS * P)
    r_f, r_b = ar.take(LEVELS * P), ar.take(LEVELS * P)
    masked, pT = ar.take(NMASK * P), ar.take(P)
    dec_e = ar.take(2 * P)
    q_f, k_d, k_t = ar.take(P), ar.take(P), ar.take(P)
    q_b = ar.take(T)
    s_f = [ar.take(GLA_DV) for _ in range(2)]
    s_b = ar.take(CHUNKS * GLA_DV).rearrange("p (n v) -> p n v", n=CHUNKS)
    o = ar.take(DV2 * T).rearrange("p (v t) -> p v t", v=DV2)
    sq = soft.rearrange("p (v t) -> p v t", v=DV2)
    ms, r, tmp = la[:, 0:T], la[:, T:2 * T], masked[:, 0:T]
    sg = v.rearrange("p n v -> p (n v)").rearrange("p (v t) -> p v t", v=DV2)
    ngain = ar.take(DV2)
    ps = B.ps

    names = ("const_in", "w_in", "w_used", "lo_mm", "lo_ev", "z_mm", "z_act", "la_ok", "m_mm", "m_ev", "v_mm", "v_ev",
             "eb_mm", "eb_ok", "kd_ok", "kt_mm", "kt_ok", "st_mm", "st_ok",
             "ex_mm", "ex_ok", "rf_ok", "rb_ok", "sc_mm", "pt_ok", "fkt_mm", "fkt_ok", "fst_mm", "fst_ok",
             "o_mm", "o_ev", "sq_ok", "ms_mm", "ms_ok", "root_ok", "silu_ok", "head_ok", "dve_chain", "act_chain")
    (const_in, w_in, w_used, lo_mm, lo_ev, z_mm, z_act, la_ok, m_mm, m_ev, v_mm, v_ev,
     eb_mm, eb_ok, kd_ok, kt_mm, kt_ok, st_mm, st_ok,
     ex_mm, ex_ok, rf_ok, rb_ok, sc_mm, pt_ok, fkt_mm, fkt_ok, fst_mm, fst_ok,
     o_mm, o_ev, sq_ok, ms_mm, ms_ok, root_ok, silu_ok, head_ok, dve_chain, act_chain) = (B.sem("gla_" + x) for x in names)
    NB = len(BACKWARD) - 1
    scale = P ** -0.5

    def block(ap, level, half):
        return ap.rearrange("p (n two w) -> p n two w", two=2, w=1 << level)[:, :, half, :]

    def sync(sp):
        sp.dma_start(sums[0], B.a["range_sums"][0]).then_inc(const_in, 16)
        sp.dma_start(sums[1], B.a["range_sums"][1]).then_inc(const_in, 16)
        sp.dma_start(masks, B.a["gla_masks"]).then_inc(const_in, 16)
        sp.dma_start(wlo, B.a["gla_w_lo"]).then_inc(const_in, 16)
        sp.dma_start(walpha[0:GLA_RANK + 1], B.a["gla_w_alpha"]).then_inc(const_in, 16)
        sp.dma_start(lo[GLA_RANK:GLA_RANK + 1], B.a["ones_row"]).then_inc(const_in, 16)
        sp.dma_start(ngain, B.a["gla_norm_g"]).then_inc(const_in, 16)
        with sp.Fori(0, H) as i:
            sp.wait_ge(w_used, i + 1)
            sp.dma_start(wqkg, B.a["gla_w_qkg"][ds(i, 1)].squeeze(0)).then_inc(w_in, 16)
            sp.dma_start(wv, B.a["gla_w_v"][ds(i, 1)].squeeze(0)).then_inc(w_in, 16)

    def tensor(pe):
        pe.wait_ge(const_in, 7 * 16)
        for d in range(2):
            for n, (s0, m, _) in enumerate((CTX, LAT)):
                for c in range(C):
                    mm = pe.matmul(ps[0:GLA_RANK, 2 * d + n, 0:m], wlo[:, c, d * GLA_RANK:(d + 1) * GLA_RANK],
                                   B.x[:, c, s0:s0 + m], start=c == 0, stop=c == C - 1)
        mm.then_inc(lo_mm, 1)
        pe.wait_ge(lo_ev, 1)
        pe.sem_inc(w_used, 1)
        with pe.Fori(0, H) as i:
            for n in range(2 * CHUNKS):
                d, c = divmod(n, CHUNKS)
                mm = pe.matmul(ps[:, 5 + n // 4, n % 4 * P:n % 4 * P + P], lo[0:GLA_RANK + 1, d, c * P:c * P + P],
                               walpha[0:GLA_RANK + 1, d, ds(i * P, P)], start=True, stop=True)
            mm.then_inc(z_mm, 1)
            pe.wait_ge(w_in, 32 * i + 32)
            for m in range(4):
                if m >= 2:
                    pe.wait_ge(m_ev, 4 * i + m - 1)
                for n, (s0, w, _) in enumerate((CTX, LAT)):
                    for c in range(C):
                        mm = pe.matmul(ps[:, m % 2 * 2 + n, 0:w], wqkg[:, c, m * P:m * P + P],
                                       B.x[:, c, s0:s0 + w], start=c == 0, stop=c == C - 1)
                mm.then_inc(m_mm, 1)
            pe.wait_ge(la_ok, i + 1)
            for t in range(CHUNKS):
                for c in range(C):
                    mm = pe.matmul(ps[:, 5 + t // 2, t % 2 * 256:t % 2 * 256 + 256], B.x[:, c, t * P:t * P + P],
                                   wv[:, c, :], start=c == 0, stop=c == C - 1)
            mm.then_inc(v_mm, 1)
            pe.wait_ge(v_mm, i + 1)
            pe.sem_inc(w_used, 1)
            pe.wait_ge(v_ev, i + 1)
            pe.wait_ge(m_ev, 4 * i + 4)
            for s, c in enumerate(BACKWARD):
                pe.matmul(ps[:, s % 2, 0:2 * P], la[:, (CHUNKS + c) * P:(CHUNKS + c + 1) * P],
                          sums[1][:, LEVELS * P:], start=True, stop=True).then_inc(eb_mm, 1)
                if s < NB:
                    pe.wait_ge(kd_ok, NB * i + s + 1)
                    pe.transpose(ps[:, 2, 0:P], k_d, B.ident[:, :]).then_inc(kt_mm, 1)
                    pe.wait_ge(kt_ok, NB * i + s + 1)
                    pe.matmul(ps[:, 3, 0:GLA_DV], k_t, v[:, c, :], start=True, stop=True).then_inc(st_mm, 1)
            pe.wait_ge(st_ok, NB * i + NB)
            pe.wait_ge(eb_ok, CHUNKS * i + CHUNKS)
            for c in FORWARD:
                if c:
                    pe.wait_ge(pt_ok, CHUNKS * i + c)
                for n in range(3):
                    pe.matmul(ps[:, n, 0:384], la[:, c * P:c * P + P], sums[0][:, n * 384:n * 384 + 384],
                              start=True, stop=True)
                for n in range(2):
                    mm = pe.matmul(ps[:, 3 + n, 0:448], la[:, (CHUNKS + c) * P:(CHUNKS + c + 1) * P],
                                   sums[1][:, n * 448:n * 448 + 448], start=True, stop=True)
                mm.then_inc(ex_mm, 1)
                pe.wait_ge(rf_ok, CHUNKS * i + c + 1)
                pe.wait_ge(ex_ok, 2 * CHUNKS * i + 2 * c + 2)
                pe.matmul(ps[:, 3, 2 * P:3 * P], k[:, c * P:c * P + P], q[:, c * P:c * P + P], start=True, stop=True)
                for n in range(LEVELS):
                    pe.matmul(ps[:, n // 4, n % 4 * P:n % 4 * P + P], r_f[:, n * P:n * P + P], r_f[:, n * P:n * P + P],
                              start=True, stop=True)
                if c < CHUNKS - 1:
                    pe.transpose(ps[:, 5, 0:P], k_d, B.ident[:, :]).then_inc(fkt_mm, 1)
                pe.wait_ge(rb_ok, CHUNKS * i + c + 1)
                for n in range(LEVELS, 2 * LEVELS):
                    rb = r_b[:, (n - LEVELS) * P:(n - LEVELS + 1) * P]
                    mm = pe.matmul(ps[:, n // 4, n % 4 * P:n % 4 * P + P], rb, rb, start=True, stop=True)
                mm.then_inc(sc_mm, 1)
                if c < CHUNKS - 1:
                    pe.wait_ge(fkt_ok, (CHUNKS - 1) * i + c + 1)
                    pe.matmul(ps[:, 6, 0:GLA_DV], k_t, v[:, c, :], start=True, stop=True).then_inc(fst_mm, 1)
                pe.wait_ge(pt_ok, CHUNKS * i + c + 1)
                if c:
                    pe.wait_ge(fst_ok, (CHUNKS - 1) * i + c)
                    pe.wait_ge(o_ev, CHUNKS * i + c)
                for n in range(DV2):
                    half = slice(n * P, n * P + P)
                    more = [(v[:, c, half], pT)]
                    if c:
                        more.append((s_f[c % 2][:, half], q_f))
                    if c != BACKWARD[0]:
                        more.append((s_b[:, c, half], q_b[:, c * P:c * P + P]))
                    for m, (left, right) in enumerate(more):
                        mm = pe.matmul(ps[:, 7, half], left, right, start=m == 0, stop=m == len(more) - 1)
                mm.then_inc(o_mm, 1)
            pe.wait_ge(sq_ok, i + 1)
            for n, (s0, m, _) in enumerate((CTX, LAT)):
                for h in range(DV2):
                    mm = pe.matmul(ps[:, n, 0:m], B.ones[:, :], sq[:, h, s0:s0 + m], start=h == 0, stop=h == DV2 - 1)
            mm.then_inc(ms_mm, 1)
            pe.wait_ge(ms_ok, i + 1)

    def scalar(act):
        chain = Chain(act_chain)
        act.wait_ge(lo_mm, 1)
        for d in range(2):
            for n, (s0, m, _) in enumerate((CTX, LAT)):
                ins = act.copy(lo[0:GLA_RANK, d, s0:s0 + m], ps[0:GLA_RANK, 2 * d + n, 0:m])
        ins.then_inc(lo_ev, 1)
        with act.Fori(0, H) as i:
            chain.loop(i, 2)
            act.wait_ge(z_mm, i + 1)
            chain.done(act, act.activation(soft, ps[:, 5:8, :].rearrange("p b n -> p (b n)"), ACT.Abs))
            chain.done(act, act.activation(soft, soft, ACT.Exp, scale=-1.0))
            act.activation(soft, soft, ACT.Ln, bias=1.0).then_inc(z_act, 1)
            for m in range(4):
                act.wait_ge(m_mm, 4 * i + m + 1)
                for n, (s0, w, _) in enumerate((CTX, LAT)):
                    to = (q, k, g[:, 0, :], g[:, 1, :])[m][:, s0:s0 + w]
                    ins = act.mul(to, ps[:, m % 2 * 2 + n, 0:w], scale if m == 0 else 1.0)
                ins.then_inc(m_ev, 1)
            act.wait_ge(v_mm, i + 1)
            act.wait_ge(head_ok, i + 1)
            act.copy(v.rearrange("p n v -> p (n v)"), ps[:, 5:8, :].rearrange("p b n -> p (b n)")).then_inc(v_ev, 1)
            for s in range(CHUNKS):
                act.wait_ge(eb_mm, CHUNKS * i + s + 1)
                if s:
                    act.wait_ge(st_ok, NB * i + s)
                act.activation(dec_e, ps[:, s % 2, 0:2 * P], ACT.Exp, scale=1.0 / GLA_TAU).then_inc(eb_ok, 1)
                if s < NB:
                    act.wait_ge(kt_mm, NB * i + s + 1)
                    act.copy(k_t, ps[:, 2, 0:P]).then_inc(kt_ok, 1)
            for c in range(CHUNKS):
                act.wait_ge(ex_mm, CHUNKS * i + c + 1)
                if c:
                    act.wait_ge(rf_ok, CHUNKS * i + c)
                    act.wait_ge(rb_ok, CHUNKS * i + c)
                    act.wait_ge(fst_ok, (CHUNKS - 1) * i + c)
                act.activation(dec_f.rearrange("p (b n) -> p b n", b=3), ps[:, 0:3, 0:384], ACT.Exp,
                               scale=1.0 / GLA_TAU).then_inc(ex_ok, 1)
                act.activation(dec_b.rearrange("p (b n) -> p b n", b=2), ps[:, 3:5, 0:448], ACT.Exp,
                               scale=1.0 / GLA_TAU).then_inc(ex_ok, 1)
                if c < CHUNKS - 1:
                    act.wait_ge(fkt_mm, (CHUNKS - 1) * i + c + 1)
                    act.copy(k_t, ps[:, 5, 0:P]).then_inc(fkt_ok, 1)
                act.wait_ge(o_mm, CHUNKS * i + c + 1)
                act.copy(o[:, :, c * P:c * P + P], ps[:, 7, 0:GLA_DV].rearrange("p (v t) -> p v t", v=DV2)).then_inc(o_ev, 1)
            act.wait_ge(o_ev, CHUNKS * i + CHUNKS)
            act.activation(sq, o, ACT.Square).then_inc(sq_ok, 1)
            act.activation(sg, g, ACT.Silu).then_inc(silu_ok, 1)
            act.wait_ge(ms_ok, i + 1)
            act.activation(r, ms, ACT.Sqrt).then_inc(root_ok, 1)
        chain.end(H)

    def vector(dve):
        chain = Chain(dve_chain)
        dve.wait_ge(const_in, 7 * 16)
        dve.sem_inc(head_ok, 1)
        with dve.Fori(0, H) as i:
            chain.loop(i, 15)
            dve.wait_ge(z_act, i + 1)
            dve.scalar_tensor_tensor(out=la, in0=ps[:, 5:8, :].rearrange("p b n -> p (b n)"), scalar=0.0, in1=soft,
                                     op0=ALU.min, op1=ALU.subtract).then_inc(la_ok, 1)
            for s, c in enumerate(BACKWARD):
                dve.wait_ge(eb_ok, CHUNKS * i + s + 1)
                if s == 0:
                    dve.wait_ge(m_ev, 4 * i + 2)
                if s < NB:
                    if s:
                        dve.wait_ge(kt_mm, NB * i + s)
                    dve.tensor_tensor(q_b[:, c * P:c * P + P], q[:, c * P:c * P + P], dec_e[:, 0:P], ALU.mult)
                    dve.tensor_tensor(k_d, k[:, c * P:c * P + P], dec_e[:, P:2 * P], ALU.mult).then_inc(kd_ok, 1)
                    dve.wait_ge(st_mm, NB * i + s + 1)
                    to = s_b[:, BACKWARD[s + 1], :]
                    if s == 0:
                        dve.tensor_copy(to, ps[:, 3, 0:GLA_DV]).then_inc(st_ok, 1)
                    else:
                        dve.wait_ge(st_ok, NB * i + s)
                        dve.scalar_tensor_tensor(out=to, in0=s_b[:, c, :], scalar=dec_e[:, 0:1],
                                                 in1=ps[:, 3, 0:GLA_DV], op0=ALU.mult, op1=ALU.add).then_inc(st_ok, 1)
                else:
                    chain.inc(dve.tensor_tensor(q_b[:, c * P:c * P + P], q[:, c * P:c * P + P], dec_e[:, 0:P], ALU.mult))
            for c in FORWARD:
                here = slice(c * P, c * P + P)
                dve.wait_ge(ex_ok, 2 * CHUNKS * i + 2 * c + 1)
                if c:
                    dve.wait_ge(sc_mm, CHUNKS * i + c)
                    dve.wait_ge(o_mm, CHUNKS * i + c)
                for n in range(LEVELS):
                    to, by = r_f[:, n * P:n * P + P], dec_f[:, n * P:n * P + P]
                    dve.tensor_tensor(block(to, n, 0), block(k[:, here], n, 0), block(by, n, 0), ALU.mult)
                    dve.tensor_tensor(block(to, n, 1), block(q[:, here], n, 1), block(by, n, 1), ALU.mult)
                dve.tensor_tensor(q_f, q[:, here], dec_f[:, TO_START * P:TO_START * P + P], ALU.mult)
                dve.tensor_tensor(k_d, k[:, here], dec_f[:, TO_END * P:TO_END * P + P], ALU.mult).then_inc(rf_ok, 1)
                dve.wait_ge(sc_mm, CHUNKS * i + c + 1)
                chain.done(dve, dve.tensor_tensor(masked, ps[:, 0:4, :].rearrange("p b n -> p (b n)")[:, 0:NMASK * P],
                                                  masks, ALU.mult))
                dve.tensor_reduce(pT, masked.rearrange("p (n i) -> p i n", n=NMASK), AX.X, ALU.add).then_inc(pt_ok, 1)
                if c < CHUNKS - 1:
                    dve.wait_ge(fst_mm, (CHUNKS - 1) * i + c + 1)
                    to = s_f[(c + 1) % 2]
                    if c == 0:
                        dve.tensor_copy(to, ps[:, 6, 0:GLA_DV]).then_inc(fst_ok, 1)
                    else:
                        dve.wait_ge(fst_ok, (CHUNKS - 1) * i + c)
                        dve.scalar_tensor_tensor(out=to, in0=s_f[c % 2], scalar=dec_f[:, TO_START * P + P - 1:TO_START * P + P],
                                                 in1=ps[:, 6, 0:GLA_DV], op0=ALU.mult, op1=ALU.add).then_inc(fst_ok, 1)
            dve.wait_ge(ms_mm, i + 1)
            dve.wait_ge(pt_ok, CHUNKS * i + CHUNKS)
            dve.tensor_scalar(ms[:, 0:NCTX], ps[:, 0, 0:NCTX], 1.0 / GLA_DV, EPS, ALU.mult, ALU.add)
            dve.tensor_scalar(ms[:, NCTX:], ps[:, 1, :], 1.0 / GLA_DV, EPS, ALU.mult, ALU.add).then_inc(ms_ok, 1)
            dve.wait_ge(root_ok, i + 1)
            chain.done(dve, dve.reciprocal(r, r))
            chain.done(dve, dve.tensor_tensor(tmp, r, r, ALU.mult))
            chain.done(dve, dve.tensor_tensor(tmp, tmp, ms, ALU.mult))
            chain.done(dve, dve.tensor_scalar(tmp, tmp, -0.5, 1.5, ALU.mult, ALU.add))
            chain.done(dve, dve.tensor_tensor(r, r, tmp, ALU.mult))
            for n in range(DV2):
                chain.inc(dve.scalar_tensor_tensor(out=o[:, n, :], in0=o[:, n, :], scalar=ngain[:, n:n + 1], in1=r,
                                                   op0=ALU.mult, op1=ALU.mult))
            dve.wait_ge(silu_ok, i + 1)
            chain.wait(dve)
            chain.inc(dve.tensor_tensor(oT[:, ds(DV2 * i, DV2), :], o, sg, ALU.mult))
            chain.wait(dve)
            dve.sem_inc(head_ok, 1)
        chain.end(H)

    def gpsimd(pool):
        with pool.Fori(0, H) as i:
            for c in FORWARD:
                here = slice(c * P, c * P + P)
                pool.wait_ge(ex_ok, 2 * CHUNKS * i + 2 * c + 2)
                for n in range(LEVELS):
                    to, by = r_b[:, n * P:n * P + P], dec_b[:, n * P:n * P + P]
                    pool.tensor_tensor(block(to, n, 0), block(q[:, here], n, 0), block(by, n, 0), ALU.mult)
                    ins = pool.tensor_tensor(block(to, n, 1), block(k[:, here], n, 1), block(by, n, 1), ALU.mult)
                ins.then_inc(rb_ok, 1)

    return {"sync": sync, "tensor": tensor, "scalar": scalar, "vector": vector, "gpsimd": gpsimd}



def project_out(B, w_dram, t_first, layer, segs):
    ar = Arena(B.mixer_arena)
    mixed = ar.take(C * T).rearrange("p (c t) -> p c t", c=C)
    w = [ar.take(C * P).rearrange("p (c n) -> p c n", c=C) for _ in range(2)]
    w_in = [B.sem(f"out_w_in{s}") for s in range(2)]
    w_used, summed, added = (B.sem(f"out_{x}") for x in ("w_used", "summed", "added"))

    def sync(sp):
        with sp.Fori(0, C // 2) as i:
            for s in range(2):
                sp.wait_ge(w_used, 2 * i + s + 1)
                sp.dma_start(w[s], w_dram[ds(2 * i + s, 1)].squeeze(0)).then_inc(w_in[s], 16)

    def tensor(pe):
        pe.sem_inc(w_used, 2)
        with pe.Fori(0, C // 2) as i:
            for s in range(2):
                pe.wait_ge(w_in[s], 16 * i + 16)
                pe.wait_ge(added, 2 * i + s + 1)
                for (s0, m, which) in segs:
                    for c in range(C):
                        mm = pe.matmul(B.ps[:, 2 * s + which, 0:m], w[s][:, c, :],
                                       mixed[:, c, s0 - t_first:s0 - t_first + m], start=c == 0, stop=c == C - 1)
                mm.then_inc(summed, 1)
                pe.wait_ge(summed, 2 * i + s + 1)
                pe.sem_inc(w_used, 1)

    def vector(dve):
        dve.sem_inc(added, 2)
        with dve.Fori(0, C // 2) as i:
            for s in range(2):
                dve.wait_ge(summed, 2 * i + s + 1)
                for (s0, m, which) in segs:
                    h = B.h[:, ds(2 * i + s, 1), s0:s0 + m]
                    ins = dve.scalar_tensor_tensor(out=h, in0=B.ps[:, 2 * s + which:2 * s + which + 1, 0:m],
                                                   scalar=B.mod[:, layer, 2, ds(2 * i + s, 1), which],
                                                   in1=h, op0=ALU.mult, op1=ALU.add)
                ins.then_inc(added, 1)

    return {"sync": sync, "tensor": tensor, "vector": vector}



def attention(B):
    QT, KT = NLAT // P, T // P
    ar = Arena(B.mixer_arena)
    mixed = ar.take(C * T).rearrange("p (c t) -> p c t", c=C)
    w = ar.take(C * 3 * P).rearrange("p (c n) -> p c n", c=C)
    cos, sin, swap = ar.take(NLAT), ar.take(NLAT), ar.take(P)
    q_raw, k_raw, turned = ar.take(NLAT), ar.take(NLAT), ar.take(2 * NLAT).rearrange("p (n t) -> p n t", n=2)
    q, k = ar.take(NLAT), ar.take(T)
    v = ar.take(T).rearrange("p (n v) -> p n v", n=KT)
    p = [[ar.take(T) for _ in range(2)] for _ in range(2)]
    aT = ar.take(KT * NLAT).rearrange("p (n t) -> p n t", n=KT)
    o, sq, ms, r, tmp = (ar.take(NLAT) for _ in range(5))
    stat = [[ar.take(8) for _ in range(2)] for _ in range(2)]
    lam_in, lam, ngain = ar.take(4 * HD), ar.take(8), ar.take(1)
    ps = B.ps
    names = ("const_in", "w_in", "w_used", "proj_mm", "proj_ev", "rot_mm", "rot_ok", "v_mm", "v_ev", "s_mm", "max_ok",
             "exp_ok", "p_ok", "at_mm", "at_ev", "o_mm", "o_ev", "sq_ok", "ms_mm", "ms_ok", "root_ok", "head_ok",
             "lam_a", "lam_b", "dve_chain")
    (const_in, w_in, w_used, proj_mm, proj_ev, rot_mm, rot_ok, v_mm, v_ev, s_mm, max_ok,
     exp_ok, p_ok, at_mm, at_ev, o_mm, o_ev, sq_ok, ms_mm, ms_ok, root_ok, head_ok,
     lam_a, lam_b, dve_chain) = (B.sem("att_" + x) for x in names)

    def sync(sp):
        for to, name in ((cos, "cos"), (sin, "sin"), (swap, "swap"), (lam_in, "diff_lambda"), (ngain, "diff_norm_g")):
            sp.dma_start(to, B.a[name]).then_inc(const_in, 16)
        with sp.Fori(0, DIFF_HEADS) as i:
            sp.wait_ge(w_used, i + 1)
            sp.dma_start(w, B.a["diff_w_in"][ds(i, 1)].squeeze(0)).then_inc(w_in, 16)

    def tensor(pe):
        pe.sem_inc(w_used, 1)
        pe.wait_ge(const_in, 5 * 16)
        with pe.Fori(0, DIFF_HEADS) as i:
            pe.wait_ge(w_in, 16 * i + 16)
            for bank, col, s0, m in ((0, 0, NCTX, NLAT), (1, P, NCTX, NLAT), (2, P, 0, NCTX)):
                for c in range(C):
                    mm = pe.matmul(ps[:, bank, 0:m], w[:, c, col:col + P], B.x[:, c, s0:s0 + m],
                                   start=c == 0, stop=c == C - 1)
            mm.then_inc(proj_mm, 1)
            for t in range(KT):
                for c in range(C):
                    mm = pe.matmul(ps[:, 3 + t // 4, t % 4 * P:t % 4 * P + P], B.x[:, c, t * P:t * P + P],
                                   w[:, c, 2 * P:3 * P], start=c == 0, stop=c == C - 1)
            mm.then_inc(v_mm, 1)
            pe.wait_ge(v_mm, i + 1)
            pe.sem_inc(w_used, 1)
            pe.wait_ge(proj_ev, i + 1)
            for n, raw in enumerate((q_raw, k_raw)):
                mm = pe.matmul(ps[:, 5 + n, :], swap, raw, start=True, stop=True)
            mm.then_inc(rot_mm, 1)
            pe.wait_ge(rot_ok, i + 1)
            pe.wait_ge(v_ev, i + 1)

            def scores(t):
                for m in range(2):
                    for n in range(2):
                        mm = pe.matmul(ps[:, 2 * m + n, 0:384], q[m * HD:m * HD + HD, t * P:t * P + P],
                                       k[m * HD:m * HD + HD, n * 384:n * 384 + 384], start=True, stop=True)
                    mm.then_inc(s_mm, 1)

            scores(0)
            for t in range(QT):
                if t + 1 < QT:
                    pe.wait_ge(exp_ok, 2 * QT * i + 2 * t + 2)
                    scores(t + 1)
                pe.wait_ge(p_ok, QT * i + t + 1)
                if t:
                    pe.wait_ge(at_ev, QT * i + t)
                for n in range(KT):
                    mm = pe.transpose(ps[:, 4 + n // 4, n % 4 * P:n % 4 * P + P], p[t % 2][0][:, n * P:n * P + P],
                                      B.ident[:, :])
                mm.then_inc(at_mm, 1)
            pe.wait_ge(at_ev, QT * i + QT)
            for n in range(KT):
                mm = pe.matmul(ps[:, 6, :], v[:, n, :], aT[:, n, :], start=n == 0, stop=n == KT - 1)
            mm.then_inc(o_mm, 1)
            pe.wait_ge(sq_ok, i + 1)
            pe.matmul(ps[:, 7, :], B.ones[:, :], sq, start=True, stop=True).then_inc(ms_mm, 1)

    def scalar(act):
        act.wait_ge(lam_a, 1)
        act.activation(lam[:, 2:4], lam[:, 0:2], ACT.Exp).then_inc(lam_b, 1)
        with act.Fori(0, DIFF_HEADS) as i:
            act.wait_ge(proj_mm, i + 1)
            act.wait_ge(head_ok, i + 1)
            act.copy(q_raw, ps[:, 0, :])
            act.copy(k_raw, ps[:, 1, :])
            act.copy(k[:, 0:NCTX], ps[:, 2, 0:NCTX]).then_inc(proj_ev, 1)
            act.wait_ge(v_mm, i + 1)
            act.copy(v[:, 0:4, :].rearrange("p n v -> p (n v)"), ps[:, 3, :])
            act.copy(v[:, 4:6, :].rearrange("p n v -> p (n v)"), ps[:, 4, 0:2 * P]).then_inc(v_ev, 1)
            for t in range(QT):
                if t >= 2:
                    act.wait_ge(at_mm, QT * i + t - 1)
                for m in range(2):
                    act.wait_ge(max_ok, 2 * QT * i + 2 * t + m + 1)
                    act.activation(p[t % 2][m].rearrange("p (n k) -> p n k", n=2), ps[:, 2 * m:2 * m + 2, 0:384], ACT.Exp,
                                   bias=stat[t % 2][m][:, 1:2], scale=HD ** -0.5,
                                   accum_out=stat[t % 2][m][:, 2:3]).then_inc(exp_ok, 1)
                act.wait_ge(at_mm, QT * i + t + 1)
                act.copy(aT[:, 0:4, t * P:t * P + P], ps[:, 4, :].rearrange("p (n k) -> p n k", n=4))
                act.copy(aT[:, 4:6, t * P:t * P + P], ps[:, 5, 0:2 * P].rearrange("p (n k) -> p n k", n=2)).then_inc(at_ev, 1)
            act.wait_ge(o_mm, i + 1)
            act.copy(o, ps[:, 6, :]).then_inc(o_ev, 1)
            act.activation(sq, ps[:, 6, :], ACT.Square).then_inc(sq_ok, 1)
            act.wait_ge(ms_ok, i + 1)
            act.activation(r, ms, ACT.Sqrt).then_inc(root_ok, 1)

    def vector(dve):
        chain = Chain(dve_chain)
        dve.wait_ge(const_in, 5 * 16)
        for n in range(2):
            at = 2 * n * HD
            chain.done(dve, dve.tensor_tensor(tmp[:, 0:HD], lam_in[:, at:at + HD], lam_in[:, at + HD:at + 2 * HD], ALU.mult))
            chain.done(dve, dve.tensor_reduce(lam[:, n:n + 1], tmp[:, 0:HD], AX.X, ALU.add))
        dve.sem_inc(lam_a, 1)
        dve.wait_ge(lam_b, 1)
        chain.done(dve, dve.tensor_tensor(lam[:, 4:5], lam[:, 3:4], lam[:, 2:3], ALU.subtract))
        chain.done(dve, dve.tensor_scalar(lam[:, 4:5], lam[:, 4:5], -LAMBDA_INIT, None, ALU.add))
        chain.done(dve, dve.tensor_scalar(ngain, ngain, 1.0 - LAMBDA_INIT, None, ALU.mult))
        chain.base, chain.n = chain.n, 0
        dve.sem_inc(head_ok, 1)
        with dve.Fori(0, DIFF_HEADS) as i:
            chain.loop(i, 4 + 5 * QT + 5)
            dve.wait_ge(proj_ev, i + 1)
            dve.wait_ge(rot_mm, i + 1)
            for n in range(2):
                chain.inc(dve.tensor_tensor(turned[:, n, :], ps[:, 5 + n, :], sin, ALU.mult))
            for n, raw in enumerate((q_raw, k_raw)):
                chain.inc(dve.tensor_tensor(raw, raw, cos, ALU.mult))
            chain.wait(dve)
            dve.tensor_tensor(q, q_raw, turned[:, 0, :], ALU.add)
            dve.tensor_tensor(k[:, NCTX:], k_raw, turned[:, 1, :], ALU.add).then_inc(rot_ok, 1)

            def maxima(t):
                for m in range(2):
                    st = stat[t % 2][m]
                    dve.wait_ge(s_mm, 2 * QT * i + 2 * t + m + 1)
                    chain.done(dve, dve.tensor_reduce(st[:, 0:1], ps[:, 2 * m:2 * m + 2, 0:384], AX.XY, ALU.max))
                    dve.tensor_scalar(st[:, 1:2], st[:, 0:1], -HD ** -0.5, None, ALU.mult).then_inc(max_ok, 1)

            maxima(0)
            for t in range(QT):
                if t + 1 < QT:
                    maxima(t + 1)
                s0, s1 = stat[t % 2]
                dve.wait_ge(exp_ok, 2 * QT * i + 2 * t + 2)
                chain.inc(dve.reciprocal(s0[:, 3:4], s0[:, 2:3]))
                chain.done(dve, dve.reciprocal(s1[:, 3:4], s1[:, 2:3]))
                chain.inc(dve.tensor_scalar(p[t % 2][1], p[t % 2][1], s1[:, 3:4], lam[:, 4:5], ALU.mult, ALU.mult))
                chain.wait(dve)
                dve.scalar_tensor_tensor(out=p[t % 2][0], in0=p[t % 2][0], scalar=s0[:, 3:4], in1=p[t % 2][1],
                                         op0=ALU.mult, op1=ALU.add).then_inc(p_ok, 1)
            dve.wait_ge(ms_mm, i + 1)
            dve.tensor_scalar(ms, ps[:, 7, :], 1.0 / (2 * HD), EPS, ALU.mult, ALU.add).then_inc(ms_ok, 1)
            dve.wait_ge(root_ok, i + 1)
            chain.done(dve, dve.reciprocal(r, r))
            chain.done(dve, dve.tensor_tensor(tmp, r, r, ALU.mult))
            chain.done(dve, dve.tensor_tensor(tmp, tmp, ms, ALU.mult))
            chain.done(dve, dve.tensor_scalar(tmp, tmp, -0.5, 1.5, ALU.mult, ALU.add))
            chain.done(dve, dve.tensor_tensor(r, r, tmp, ALU.mult))
            dve.scalar_tensor_tensor(out=mixed[:, ds(i, 1), 0:NLAT].squeeze(1), in0=o, scalar=ngain[:, 0:1], in1=r,
                                     op0=ALU.mult, op1=ALU.mult).then_inc(head_ok, 1)
        chain.end(DIFF_HEADS)

    return {"sync": sync, "tensor": tensor, "scalar": scalar, "vector": vector}



def chosen_of(B, tiles):
    return [c[:, 0:tiles * PAIRS].rearrange("p (n k) -> p n k", n=tiles) for c in B.chosen]


def product_keys(B, layer, segs):
    t0, n_tok = segs[0][0], sum(seg[1] for seg in segs)
    tiles = n_tok // P
    ar, chosen = Arena(B.gate_arena), chosen_of(B, tiles)
    w = [ar.take(C * P).rearrange("p (c n) -> p c n", c=C) for _ in range(2)]
    keys = ar.take(2 * P).rearrange("p (z k) -> p z k", z=2)
    q = [ar.take(T) for _ in range(2)]
    top = ar.take(tiles * 16 * TOPK).rearrange("p (n h z k) -> p n h z k", n=tiles, h=HEADS, z=2)
    top_i = ar.take(tiles * 16 * TOPK).rearrange("p (n h z k) -> p n h z k", n=tiles, h=HEADS, z=2)
    rest = ar.take(tiles * P).rearrange("p (n k) -> p n k", n=tiles)
    cand = ar.take(HEADS * 256).rearrange("p (h k) -> p h k", h=HEADS)
    cand2 = ar.take(HEADS * 256).rearrange("p (h k) -> p h k", h=HEADS)
    best = ar.take(PAIRS).rearrange("p (h k) -> p h k", h=HEADS)
    best_j = ar.take(PAIRS, U32).rearrange("p (h k) -> p h k", h=HEADS)
    digit_u = [ar.take(PAIRS, U32) for _ in range(2)]
    digit = [ar.take(PAIRS) for _ in range(2)]
    eq = ar.take(PAIRS * TOPK).rearrange("p (h k a) -> p h k a", h=HEADS, k=TOPK)
    soft = ar.take(PAIRS).rearrange("p (h k) -> p h k", h=HEADS)
    total, inv = ar.take(HEADS), ar.take(HEADS)
    found = ar.take(tiles * TOPK).rearrange("p (n k) -> p n k", n=tiles)
    found_i = ar.take(tiles * TOPK, U32).rearrange("p (n k) -> p n k", n=tiles)
    picked = [ar.take(PAIRS).rearrange("p (h k) -> p h k", h=HEADS) for _ in range(2)]
    passed = B.sem(f"keys_passed")

    def settle(dve):
        dve.sem_inc(passed, 1)

    iota = ar.take(TOPK)
    w_in = [B.sem(f"keys_wq_in{s}") for s in range(2)]
    (const_in, w_used, q_mm, q_ev, s_mm, s_ev, chain_s, shifted, exp_ok) = (
        B.sem(f"keys_{x}") for x in ("keys_in", "wq_used", "q_mm", "q_ev", "s_mm", "s_ev", "key_chain", "shifted", "exp_ok"))
    ps = B.ps

    def sync(sp):
        sp.dma_start(keys, B.a["subkeys"][layer]).then_inc(const_in, 16)
        sp.dma_start(iota, B.a["iota"][:, 0:TOPK]).then_inc(const_in, 16)
        with sp.Fori(0, HEADS) as i:
            for z in range(2):
                sp.wait_ge(w_used, 2 * i + z + 1)
                sp.dma_start(w[z], B.a["peer_wq"][layer, ds(2 * i + z, 1)].squeeze(0)).then_inc(w_in[z], 16)

    def tensor(pe):
        pe.sem_inc(w_used, 2)
        pe.wait_ge(const_in, 32)
        with pe.Fori(0, HEADS) as i:
            for z in range(2):
                pe.wait_ge(w_in[z], 16 * i + 16)
                pe.wait_ge(q_ev, 2 * i + z + 1)
                for (s0, m, which) in segs:
                    for c in range(C):
                        mm = pe.matmul(ps[:, which, 0:m], w[z][:, c, :], B.x[:, c, s0:s0 + m],
                                       start=c == 0, stop=c == C - 1)
                mm.then_inc(q_mm, 1)
                pe.wait_ge(q_mm, 2 * i + z + 1)
                pe.sem_inc(w_used, 1)
                pe.wait_ge(q_ev, 2 * i + z + 2)
                pe.wait_ge(s_ev, 2 * i + z + 1)
                for t in range(tiles):
                    mm = pe.matmul(ps[:, 2 + 2 * z + t // 4, t % 4 * P:t % 4 * P + P],
                                   q[z][:, t * P:t * P + P], keys[:, z, :], start=True, stop=True)
                mm.then_inc(s_mm, 1)

    def scalar(act):
        act.sem_inc(q_ev, 1)
        with act.Fori(0, HEADS) as i:
            for z in range(2):
                act.wait_ge(s_ev, 2 * i + z + 1)
                act.wait_ge(q_mm, 2 * i + z + 1)
                for (s0, m, which) in segs:
                    ins = act.copy(q[z][:, s0 - t0:s0 - t0 + m], ps[:, which, 0:m])
                ins.then_inc(q_ev, 1)
        with act.Fori(0, tiles) as i:
            act.wait_ge(shifted, i + 1)
            act.activation(soft, soft, ACT.Exp).then_inc(exp_ok, 1)

    def vector(dve):
        chain = Chain(chain_s)
        dve.sem_inc(s_ev, 2)
        dve.wait_ge(const_in, 32)
        with dve.Fori(0, HEADS) as i:
            chain.loop(i, 2 * (5 * tiles + 2))
            for z in range(2):
                dve.wait_ge(s_mm, 2 * i + z + 1)
                scores = [ps[:, 2 + 2 * z + t // 4, t % 4 * P:t % 4 * P + P] for t in range(tiles)]
                first = [found[:, t, 0:8] for t in range(tiles)]
                last = [found[:, t, 8:16] for t in range(tiles)]
                settle(dve)
                for t in range(tiles):
                    chain.inc(dve.max(first[t], scores[t]))
                chain.wait(dve)
                settle(dve)
                for t in range(tiles):
                    chain.inc(dve.max_index(found_i[:, t, 0:8], first[t], scores[t]))
                    chain.inc(dve.match_replace(rest[:, t, :], first[t], scores[t], LOWEST))
                chain.wait(dve)
                dve.sem_inc(s_ev, 1)
                for t in range(tiles):
                    chain.inc(dve.max(last[t], rest[:, t, :]))
                chain.wait(dve)
                settle(dve)
                for t in range(tiles):
                    chain.inc(dve.max_index(found_i[:, t, 8:16], last[t], rest[:, t, :]))
                chain.wait(dve)
                chain.inc(dve.tensor_scalar(top[:, :, ds(i, 1), z, :].squeeze(2), found, 0.0, None, ALU.add))
                chain.inc(dve.tensor_scalar(top_i[:, :, ds(i, 1), z, :].squeeze(2), found_i, 0.0, None, ALU.add))
                chain.wait(dve)
        chain.end(HEADS)
        with dve.Fori(0, tiles) as i:
            chain.loop(i, 57)
            tile = ds(i, 1)
            sums = cand.rearrange("p h (a b) -> p h a b", a=TOPK)
            here, here_i = top[:, tile].squeeze(1), top_i[:, tile].squeeze(1)
            chain.done(dve, dve.tensor_tensor(
                sums, here[:, :, 0, :].unsqueeze(3).to_broadcast([P, HEADS, TOPK, TOPK]),
                here[:, :, 1, :].unsqueeze(2).to_broadcast([P, HEADS, TOPK, TOPK]), ALU.add))
            settle(dve)
            for h in range(HEADS):
                chain.inc(dve.max(best[:, h, 0:8], cand[:, h, :]))
            chain.wait(dve)
            settle(dve)
            for h in range(HEADS):
                chain.inc(dve.max_index(best_j[:, h, 0:8], best[:, h, 0:8], cand[:, h, :]))
                chain.inc(dve.match_replace(cand2[:, h, :], best[:, h, 0:8], cand[:, h, :], LOWEST))
            chain.wait(dve)
            settle(dve)
            for h in range(HEADS):
                chain.inc(dve.max(best[:, h, 8:16], cand2[:, h, :]))
            chain.wait(dve)
            settle(dve)
            for h in range(HEADS):
                chain.inc(dve.max_index(best_j[:, h, 8:16], best[:, h, 8:16], cand2[:, h, :]))
            chain.inc(dve.tensor_tensor(soft, best, best[:, :, 0:1].to_broadcast([P, HEADS, TOPK]), ALU.subtract))
            chain.wait(dve)
            dve.sem_inc(shifted, 1)
            jj = best_j.rearrange("p h k -> p (h k)")
            chain.inc(dve.tensor_scalar(digit_u[0], jj, 4, None, ALU.logical_shift_right))
            chain.inc(dve.tensor_scalar(digit_u[1], jj, TOPK - 1, None, ALU.bitwise_and))
            chain.wait(dve)
            for z in range(2):
                chain.inc(dve.tensor_copy(digit[z], digit_u[z]))
            for z in range(2):
                chain.wait(dve)
                chain.done(dve, dve.tensor_tensor(
                    eq.rearrange("p h k a -> p (h k) a"), digit[z].unsqueeze(2).to_broadcast([P, PAIRS, TOPK]),
                    iota.unsqueeze(1).to_broadcast([P, PAIRS, TOPK]), ALU.is_equal))
                chain.done(dve, dve.tensor_tensor(
                    eq, eq, here_i[:, :, z, :].unsqueeze(2).to_broadcast([P, HEADS, TOPK, TOPK]), ALU.mult))
                chain.done(dve, dve.tensor_reduce(picked[z], eq, AX.X, ALU.add))
                chain.inc(dve.tensor_scalar(chosen[z][:, tile, :].squeeze(1).rearrange("p (h k) -> p h k", h=HEADS),
                                            picked[z], 0.0, None, ALU.add))
            dve.wait_ge(exp_ok, i + 1)
            chain.done(dve, dve.tensor_reduce(total, soft, AX.X, ALU.add))
            chain.done(dve, dve.reciprocal(inv, total))
            chain.done(dve, dve.tensor_tensor(chosen[2][:, tile, :].squeeze(1).rearrange("p (h k) -> p h k", h=HEADS), soft,
                                              inv.unsqueeze(2).to_broadcast([P, HEADS, TOPK]), ALU.mult))
        chain.end(tiles)

    return {"sync": sync, "tensor": tensor, "scalar": scalar, "vector": vector}


def gates(B, segs):
    t0, n_tok = segs[0][0], sum(seg[1] for seg in segs)
    tiles = n_tok // P
    ar, chosen = Arena(B.gate_arena), chosen_of(B, tiles)
    turned = [ar.take(P) for _ in range(3)]
    iota = ar.take(P)
    row = [[ar.take(P) for _ in range(QUAD)] for _ in range(2)]
    col = [[ar.take(P) for _ in range(QUAD)] for _ in range(2)]
    out = [ar.take(KEYS * TG).rearrange("p (j t) -> p j t", j=KEYS) for _ in range(2)]
    QG = TG // QUAD
    names = ("iota_in", "turn_mm", "turn_ev", "rows_ok", "g_mm", "g_ev", "g_out0", "g_out1")
    iota_in, turn_mm, turn_ev, rows_ok, g_mm, g_ev, g_out0, g_out1 = (B.sem(f"gates_{x}") for x in names)
    g_out = (g_out0, g_out1)
    ps = B.ps

    def sync(sp):
        sp.dma_start(iota, B.a["iota"]).then_inc(iota_in, 16)
        with sp.Fori(0, tiles) as i:
            for s in range(2):
                sp.wait_ge(g_ev, 2 * QG * i + QG * (s + 1) + 2)
                sp.dma_start(B.g_dram[ds(2 * i + s, 1)].squeeze(0), out[s].rearrange("p j t -> p (j t)")).then_inc(g_out[s], 16)
        for s in range(2):
            sp.wait_ge(g_out[s], 16 * tiles + 16)

    chosen_now = [ar.take(P) for _ in range(3)]
    now_ok = B.sem(f"gates_now_ok")

    def tensor(pe):
        with pe.Fori(0, tiles) as i:
            pe.wait_ge(now_ok, i + 1)
            for n in range(3):
                mm = pe.transpose(ps[:, 4, n * P:n * P + P], chosen_now[n], B.ident[:, :])
            mm.then_inc(turn_mm, 1)
            for g in range(2 * QG):
                s = g % 2
                pe.wait_ge(rows_ok, 2 * QG * i + g + 1)
                pe.wait_ge(g_ev, 2 * QG * i + g + 1)
                for n in range(QUAD):
                    mm = pe.matmul(ps[:, s, n * P:n * P + P], row[s][n], col[s][n], start=True, stop=True)
                mm.then_inc(g_mm, 1)

    def scalar(act):
        act.sem_inc(g_ev, 2)
        act.sem_inc(g_out0, 16)
        act.sem_inc(g_out1, 16)
        with act.Fori(0, tiles) as i:
            for g in range(2 * QG):
                s, half, at = g % 2, g // QG, g % QG * QUAD
                if g % QG == 0:
                    act.wait_ge(g_out[half], 16 * i + 16)
                act.wait_ge(g_mm, 2 * QG * i + g + 1)
                act.copy(out[half][:, :, at:at + QUAD].rearrange("p j t -> p t j"),
                         ps[:, s, :].rearrange("p (t j) -> p t j", t=QUAD)).then_inc(g_ev, 1)

    def vector(dve):
        dve.wait_ge(iota_in, 16)
        with dve.Fori(0, tiles) as i:
            for n in range(3):
                ins = dve.tensor_scalar(chosen_now[n], chosen[n][:, ds(i, 1), :].squeeze(1), 0.0, None, ALU.add)
            ins.then_inc(now_ok, 1)
            dve.wait_ge(turn_mm, i + 1)
            for n in range(3):
                ins = dve.tensor_copy(turned[n], ps[:, 4, n * P:n * P + P])
            ins.then_inc(turn_ev, 1)
            dve.wait_ge(turn_ev, i + 1)
            for g in range(2 * QG):
                s = g % 2
                if g >= 2:
                    dve.wait_ge(g_mm, 2 * QG * i + g - 1)
                for n in range(QUAD):
                    t = g * QUAD + n
                    dve.tensor_scalar(row[s][n], iota, turned[0][:, t:t + 1], None, ALU.is_equal)
                    ins = dve.tensor_scalar(col[s][n], iota, turned[1][:, t:t + 1], turned[2][:, t:t + 1],
                                            ALU.is_equal, ALU.mult)
                ins.then_inc(rows_ok, 1)
            dve.wait_ge(g_mm, 2 * QG * i + 2 * QG)

    return {"sync": sync, "tensor": tensor, "scalar": scalar, "vector": vector}


def experts(B, layer, segs):
    t0, n_tok = segs[0][0], sum(seg[1] for seg in segs)
    NG = n_tok // TG
    PAIRN = KEYS // 2
    PASSES = ((0, 0), (0, 1), (1, 0))
    acc = B.x
    ar, parts = Arena(B.peer_arena), Arena(B.part_arena)
    u_raw = [ar.take(C * P) for _ in range(2)]
    v_raw = [ar.take(D) for _ in range(2)]
    g = [ar.take(NG * 2 * TG).rearrange("p (n j t) -> p n j t", n=NG, j=2) for _ in range(2)]
    gelu = [ar.take(n_tok) for _ in range(2)]
    wt = [ar.take(n_tok) for _ in range(2)]
    u = [parts.take(2 * C * P).rearrange("p (s c n) -> p s c n", s=2, c=C) for _ in range(2)]
    v = [parts.take(2 * D).rearrange("p (s d) -> p s d", s=2) for _ in range(2)]
    w = [parts.take(2 * n_tok).rearrange("p (s t) -> p s t", s=2) for _ in range(4)]
    u_in, v_in, g_in = ([B.sem(f"exp_{x}{s}") for s in range(2)] for x in ("u_in", "v_in", "g_in"))
    names = ("u_high", "u_split", "v_high", "v_split", "s_mm", "gelu_ok", "wt_ok", "w_high", "w_split", "y_mm", "y_ev")
    u_high, u_split, v_high, v_split, s_mm, gelu_ok, wt_ok, w_high, w_split, y_mm, y_ev = (
        B.sem(f"exp_{x}") for x in names)
    ps = B.ps
    v_dram = B.a["peer_v"][layer].rearrange("(i j) d -> i j d", j=KEYS)

    def pairs(engine, body):
        body(0, 0, True, False)
        with engine.Fori(0, PAIRN // 2 - 1) as i:
            body(2 * i + 1, 1, False, False)
            body(2 * i + 2, 0, False, False)
        body(PAIRN - 1, 1, False, True)

    def sync(sp):
        def load_v(n):
            for k in range(2):
                sp.wait_ge(v_split, 2 * n + k + 1)
                sp.dma_start(v_raw[k], v_dram[:, ds(2 * n + k, 1), :].squeeze(1)).then_inc(v_in[k], 16)

        def body(n, parity, first, last):
            for k in range(2):
                sp.wait_ge(u_split, 2 * n + k + 1)
                sp.dma_start(u_raw[k], B.a["peer_u"][layer, ds(2 * n + k, 1)].squeeze(0).rearrange(
                    "p c n -> p (c n)")).then_inc(u_in[k], 16)
            sp.wait_ge(wt_ok, 2 * n + 2)
            sp.dma_start(g[parity], B.g_dram[0:NG, :, ds(n * 2 * TG, 2 * TG)].rearrange("n i k -> i n k")).then_inc(
                g_in[parity], 16)
            if not first:
                load_v(n - 1)
            if last:
                load_v(n)

        pairs(sp, body)

    def tensor(pe):
        pe.sem_inc(s_mm, 2)
        pe.sem_inc(y_mm, C)

        def values(n, parity):
            pe.wait_ge(v_split, 2 * n + 4)
            pe.wait_ge(w_split, 2 * n + 4 + 2)
            for c in range(C):
                pe.wait_ge(y_ev, n * C + c + 1)
                for (s0, m, which) in segs:
                    todo = [(k, a, b) for k in range(2) for a, b in PASSES]
                    for at, (k, a, b) in enumerate(todo):
                        mm = pe.matmul(ps[:, 4 + 2 * (c % 2) + which, 0:m], v[k][:, a, c * P:c * P + P],
                                       w[2 * parity + k][:, b, s0 - t0:s0 - t0 + m],
                                       start=at == 0, stop=at == len(todo) - 1)
                mm.then_inc(y_mm, 1)

        def body(n, parity, first, last):
            for k in range(2):
                pe.wait_ge(u_split, 2 * n + k + 3)
                pe.wait_ge(gelu_ok, 2 * n + k + 1)
                for (s0, m, which) in segs:
                    todo = [(c, a, b) for c in range(C) for a, b in PASSES]
                    for at, (c, a, b) in enumerate(todo):
                        mm = pe.matmul(ps[:, 2 * k + which, 0:m], u[k][:, a, c, :], B.xr[:, b, c, s0:s0 + m],
                                       start=at == 0, stop=at == len(todo) - 1)
                mm.then_inc(s_mm, 1)
            if not first:
                values(n - 1, 1 - parity)
            if last:
                values(n, parity)

        pairs(pe, body)

    def scalar(act):
        act.sem_inc(gelu_ok, 2)

        def split_u(j, k):
            act.wait_ge(u_in[k], 8 * j - 8 * k + 16)
            act.wait_ge(s_mm, j + 1)
            act.copy(u[k][:, 0].rearrange("p c n -> p (c n)"), u_raw[k]).then_inc(u_high, 1)

        def split_v(n):
            for k in range(2):
                act.wait_ge(v_in[k], 16 * n + 16)
                act.wait_ge(y_mm, C * n + C)
                act.copy(v[k][:, 0], v_raw[k]).then_inc(v_high, 1)

        def weigh(n, parity, k, first):
            act.wait_ge(s_mm, 2 * n + k + 3)
            act.wait_ge(wt_ok, 2 * n + k + 3)
            for (s0, m, which) in segs:
                ins = act.activation(gelu[k][:, s0 - t0:s0 - t0 + m], ps[:, 2 * k + which, 0:m], ACT.Gelu)
            ins.then_inc(gelu_ok, 1)
            act.wait_ge(wt_ok, 2 * n + k + 5)
            if not first:
                act.wait_ge(y_mm, C * n)
            act.copy(w[2 * parity + k][:, 0], wt[k]).then_inc(w_high, 1)

        def body(n, parity, first, last):
            if first:
                split_u(0, 0)
            split_u(2 * n + 1, 1)
            if not first:
                split_v(n - 1)
            weigh(n, parity, 0, first)
            if not last:
                split_u(2 * n + 2, 0)
            weigh(n, parity, 1, first)
            if last:
                split_v(n)

        pairs(act, body)

    def gpsimd(pool):
        pool.sem_inc(v_split, 2)
        def split_v(n):
            for k in range(2):
                pool.wait_ge(v_high, 2 * n + k + 1)
                pool.tensor_tensor(v[k][:, 1], v_raw[k], v[k][:, 0].bitcast(F32), ALU.subtract).then_inc(v_split, 1)

        def body(n, parity, first, last):
            if not first:
                split_v(n - 1)
            if last:
                split_v(n)

        pairs(pool, body)

    def vector(dve):
        dve.sem_inc(u_split, 2)
        dve.sem_inc(w_split, 4)
        dve.sem_inc(y_ev, 1)
        dve.memset(acc[:, :, t0:], 0.0).then_inc(y_ev, 1)
        dve.sem_inc(wt_ok, 4)
        dve.wait_ge(y_ev, 2)

        def split_u(j, k):
            dve.wait_ge(u_high, j + 1)
            dve.tensor_tensor(u[k][:, 1].rearrange("p c n -> p (c n)"), u_raw[k],
                              u[k][:, 0].rearrange("p c n -> p (c n)").bitcast(F32), ALU.subtract).then_inc(u_split, 1)

        def weigh(n, parity, k):
            if k == 0:
                dve.wait_ge(g_in[parity], 8 * n - 8 * parity + 16)
            dve.wait_ge(gelu_ok, 2 * n + k + 3)
            dve.wait_ge(w_split, 2 * n + k + 3)
            dve.tensor_tensor(wt[k].rearrange("p (n t) -> p n t", n=NG), gelu[k].rearrange("p (n t) -> p n t", n=NG),
                              g[parity][:, :, k, :], ALU.mult).then_inc(wt_ok, 1)

        def split_w(n, parity, k):
            dve.wait_ge(w_high, 2 * n + k + 1)
            dve.tensor_tensor(w[2 * parity + k][:, 1], wt[k], w[2 * parity + k][:, 0].bitcast(F32),
                              ALU.subtract).then_inc(w_split, 1)

        def collect(n, cs):
            for c in cs:
                dve.wait_ge(y_mm, C * n + c + 1 + C)
                if c == 0:
                    dve.wait_ge(y_ev, C * n + 2)
                for (s0, m, which) in segs:
                    ins = dve.tensor_tensor(acc[:, c, s0:s0 + m], ps[:, 4 + 2 * (c % 2) + which, 0:m],
                                            acc[:, c, s0:s0 + m], ALU.add)
                ins.then_inc(y_ev, 1)

        def body(n, parity, first, last):
            if first:
                split_u(0, 0)
            split_u(2 * n + 1, 1)
            weigh(n, parity, 0)
            split_w(n, parity, 0)
            if not last:
                split_u(2 * n + 2, 0)
            weigh(n, parity, 1)
            split_w(n, parity, 1)
            if not first:
                collect(n - 1, range(C))
            if last:
                collect(n, range(C))

        pairs(dve, body)
        dve.wait_ge(y_ev, PAIRN * C + 2)
        for c in range(C):
            for (s0, m, which) in segs:
                dve.scalar_tensor_tensor(out=B.h[:, c, s0:s0 + m], in0=acc[:, c, s0:s0 + m],
                                         scalar=B.mod[:, layer, 5, c, which:which + 1], in1=B.h[:, c, s0:s0 + m],
                                         op0=ALU.mult, op1=ALU.add)

    return {"sync": sync, "tensor": tensor, "scalar": scalar, "gpsimd": gpsimd, "vector": vector}



def columns(w):
    k, m = w.shape
    return np.ascontiguousarray(w.reshape(k // P, P, m // P, P).transpose(2, 1, 0, 3))


def rows(w):
    k, m = w.shape
    return w.reshape(k // P, P, m).transpose(1, 0, 2)


def layout(i):
    f = {n: np.asarray(x) for n, x in i.items()}
    a = {}
    a["hidden"] = rows(np.concatenate([f["ctx"][0], f["x"][0]], 0).T)
    a["cond"] = rows(np.stack([f["c_ctx"], f["c"][0]], 1))
    wm = [columns(f["w_mod"][l]) for l in range(DEPTH)]
    wm = np.concatenate(wm, 0)
    a["w_mod"] = wm.reshape(-1, 4, P, C, P).transpose(0, 2, 1, 3, 4)
    a["b_mod"] = f["b_mod"].reshape(DEPTH * 6 * C, P).T
    gains = [f["norm1_g"][0], f["norm1_g"][1], f["norm2_g"][0], f["norm2_g"][1], f["final_g"]]
    a["gains"] = np.stack(gains).reshape(5 * C, P).T
    hk = GLA_HEADS * P
    w = f["gla_w_in"][0]
    q, k, v, g = w[:, :hk], w[:, hk:2 * hk], w[:, 2 * hk:2 * hk + D], w[:, 2 * hk + D:2 * hk + 2 * D]
    a["gla_w_qkg"] = np.stack([np.concatenate([rows(q[:, n * P:n * P + P]), rows(k[:, n * P:n * P + P]),
                                               rows(g[:, n * GLA_DV:(n + 1) * GLA_DV])], 2) for n in range(GLA_HEADS)])
    a["gla_w_v"] = np.stack([rows(v[:, n * GLA_DV:(n + 1) * GLA_DV]) for n in range(GLA_HEADS)])
    a["gla_w_lo"] = rows(w[:, 2 * hk + 2 * D:])
    a["gla_w_alpha"] = np.concatenate([f["gla_w_alpha"][0].transpose(1, 0, 2), f["gla_b_alpha"][0][None]], 0)
    a["gla_norm_g"] = f["gla_norm_g"][0].reshape(-1, P).T
    a["gla_w_out"] = columns(f["gla_w_out"][0])
    w = f["diff_w_in"][0]
    a["diff_w_in"] = np.stack([np.concatenate([rows(w[:, n * D + h * P:n * D + h * P + P]) for n in range(3)], 2)
                               for h in range(DIFF_HEADS)])
    a["diff_lambda"] = np.broadcast_to(f["diff_lambda"][0].reshape(1, -1), (P, 4 * HD))
    a["diff_norm_g"] = f["diff_norm_g"][0].reshape(P, 1)
    a["diff_w_out"] = columns(f["diff_w_out"][0])
    a["peer_wq"] = np.stack([columns(f["peer_wq"][l]) for l in range(DEPTH)])
    a["subkeys"] = f["peer_subkeys"].transpose(0, 3, 1, 2)
    a["peer_u"] = f["peer_u"].reshape(DEPTH, KEYS, KEYS, C, P).transpose(0, 2, 4, 3, 1)
    a["peer_v"] = f["peer_v"]
    a["ident"] = np.eye(P, dtype=np.float32)
    a["iota"] = np.broadcast_to(np.arange(P, dtype=np.float32), (P, P))
    a["ones_row"] = np.ones((1, 2, T), np.float32)
    a["range_sums"], a["gla_masks"] = gla_range_sums(), gla_masks()
    a["cos"], a["sin"], a["swap"] = rope_tables()
    return {"in_" + n: np.ascontiguousarray(x) for n, x in a.items()}


def kernel(**inputs):
    import concourse.bacc as bacc
    from concourse.bass_utils import run_bass_kernel_spmd

    nc = bacc.Bacc("TRN2", target_bir_lowering=False, num_devices=1)
    arrays = layout(inputs)
    a = {n[3:]: nc.dram_tensor(n, x.shape, mybir.dt.from_np(x.dtype), kind="ExternalInput").ap() for n, x in arrays.items()}
    out = nc.dram_tensor("out", (P, C, NLAT), F32, kind="ExternalOutput").ap()
    build(nc, a, out)
    r = run_bass_kernel_spmd(nc, [arrays], core_ids=[0])
    y = r.results[0]["out"]
    return np.ascontiguousarray(y.transpose(2, 1, 0)).reshape(1, NLAT, D)
```

```python
import math
from contextlib import ExitStack

import numpy as np
import concourse.bass as bass
from concourse import mybir
from concourse.alu_op_type import AluOpType as ALU

F32 = mybir.dt.float32
F32R = mybir.dt.float32r
U32 = mybir.dt.uint32
ACT = mybir.ActivationFunctionType
AX = mybir.AxisListType
ds = bass.ds

P = 128
D = 1024
C = D // P
NCTX = 256
NLAT = 512
T = NCTX + NLAT
CTX, LAT = (0, NCTX, 0), (NCTX, NLAT, 1)
DEPTH = 2
EPS = 1e-6

GLA_HEADS = 4
GLA_DV = D // GLA_HEADS
GLA_RANK = 16
GLA_TAU = 16.0
LEVELS = 7
TO_START, TO_END = LEVELS, LEVELS + 1
CHUNKS = T // P
CTX_CHUNKS = NCTX // P
FORWARD = list(range(CHUNKS))
BACKWARD = list(range(CTX_CHUNKS))[::-1] + list(range(CTX_CHUNKS, CHUNKS))[::-1]
NMASK = 2 * LEVELS + 1

HD = 64
DIFF_HEADS = D // (2 * HD)
GRID_W = 64
LAMBDA_INIT = 0.8 - 0.6 * math.exp(-0.3 * 1)

HEADS = 8
KEYS = 128
TOPK = 16
PAIRS = HEADS * TOPK
TG = 64
JB = 2
QUAD = 4
MIXER_ARENA = 40288
PEER_ARENA = MIXER_ARENA - 2 * C * T
PART_ARENA = 14336
LOWEST = -3.0e38



def gla_range_sums():
    m = np.zeros((2, P, LEVELS + 2, P), np.float32)
    for t in range(P):
        for level in range(LEVELS):
            b = 1 << level
            mid = t // (2 * b) * (2 * b) + b
            if t >= mid:
                m[0, mid:t + 1, level, t] = 1
                m[1, mid:t, level, t] = 1
            else:
                m[0, t + 1:mid, level, t] = 1
                m[1, t:mid, level, t] = 1
        m[0, :t + 1, TO_START, t] = 1
        m[0, t + 1:, TO_END, t] = 1
        m[1, t:, TO_START, t] = 1
        m[1, :t, TO_END, t] = 1
    return m.reshape(2, P, -1)


def gla_masks():
    m = np.zeros((P, NMASK, P), np.float32)
    for j in range(P):
        for i in range(P):
            if i == j:
                m[j, NMASK - 1, i] = 2
                continue
            level = (i ^ j).bit_length() - 1
            m[j, level if i > j else LEVELS + level, i] = 1
    return m.reshape(P, -1)


def rope_tables():
    n = HD // 4
    freqs = np.float32(10000.0) ** (-np.arange(n, dtype=np.float32) / np.float32(n))
    rows = NLAT // GRID_W
    row = np.repeat(np.arange(rows), GRID_W).astype(np.float32)
    col = np.tile(np.arange(GRID_W), rows).astype(np.float32)
    angle = np.concatenate([row[:, None] * freqs, col[:, None] * freqs], -1).astype(np.float32)
    angle = np.tile(angle.T, (P // (HD // 2), 1)).astype(np.float64)
    swap = np.zeros((P, P), np.float32)
    for p in range(P):
        if p % HD < HD // 2:
            swap[p + HD // 2, p] = -1
        else:
            swap[p - HD // 2, p] = 1
    return np.cos(angle).astype(np.float32), np.sin(angle).astype(np.float32), swap


class Names:
    pass


class Chain:

    def __init__(self, sem):
        self.sem, self.base, self.n, self.turn = sem, 0, 0, None

    def loop(self, turn, per):
        self.turn, self.per = turn, per

    def inc(self, ins):
        ins.then_inc(self.sem, 1)
        self.n += 1

    def wait(self, engine):
        at = self.base + self.n
        engine.wait_ge(self.sem, at if self.turn is None else self.turn * self.per + at)

    def done(self, engine, ins):
        self.inc(ins)
        self.wait(engine)

    def end(self, turns):
        assert self.n == self.per, self.n
        self.base += turns * self.per
        self.n, self.turn = 0, None


def build(nc, a, out):
    ctx = ExitStack()
    with ctx:
        def sem(name):
            return ctx.enter_context(nc.semaphore(name))

        def sb(name, width, dt=F32):
            return ctx.enter_context(nc.sbuf_tensor(name, [P, width], dt))

        B = Names()
        B.a, B.out = a, out
        held, B.again = {}, []

        def stage_sem(name):
            if name in held:
                B.again.append(held[name])
            else:
                held[name] = sem(name)
            return held[name]

        B.sem = stage_sem
        B.ps = ctx.enter_context(nc.psum_tensor("ps", [P, 8, 512], F32))
        B.h = sb("hidden", C * T)[:, :].rearrange("p (c t) -> p c t", c=C)
        B.x = sb("mixer_in", C * T)[:, :].rearrange("p (c t) -> p c t", c=C)
        B.mod = sb("modulation", DEPTH * 6 * C * 2)[:, :].rearrange("p (l k c s) -> p l k c s", l=DEPTH, k=6, s=2)
        small = sb("small", 4 * C + C + 5 * 2)
        B.gains = small[:, 0:5 * C].rearrange("p (n c) -> p n c", n=5)
        B.mod_bias = sb("mod_bias", DEPTH * 6 * C)[:, :]
        B.cond = sb("cond", 2 * C)[:, :].rearrange("p (c s) -> p c s", s=2)
        B.ident = sb("identity", P)
        B.ones = sb("ones", P)
        with nc.sbuf_tensor("mixer_arena", [P, MIXER_ARENA], F32) as whole:
            B.mixer_arena = whole
        B.xr = sb("ffn_in_parts", 2 * C * T, F32R)[:, :].rearrange("p (s c t) -> p s c t", s=2, c=C)
        with nc.sbuf_tensor("gate_arena", [P, PEER_ARENA], F32) as whole:
            B.gate_arena = whole
        B.part_arena = sb("part_arena", PART_ARENA, F32R)
        B.peer_arena = sb("peer_arena", PEER_ARENA - PART_ARENA)
        B.g_dram = nc.dram_tensor("gates", (T // TG, P, KEYS * TG), F32, kind="Internal").ap()

        start_in = sem("start_in")
        plan = [(modulation,)]
        for layer, segs in ((0, (CTX, LAT)), (1, (LAT,))):
            plan += [(norm, layer, B.gains[:, layer], 0, 1, (CTX, LAT)),
                     (gla,) if layer == 0 else (attention,),
                     (project_out, a["gla_w_out"] if layer == 0 else a["diff_w_out"], segs[0][0], layer, segs),
                     (norm, layer, B.gains[:, 2 + layer], 3, 4, segs, True),
                     (product_keys, layer, segs),
                     (gates, layer, segs),
                     (experts, layer, segs)]
        plan += [(norm, 1, B.gains[:, 4], None, None, (LAT,))]
        stages = []
        for make, *args in plan:
            B.again = []
            stage = make(B, *args)
            stage["again"] = B.again
            stages.append(stage)
        out_written = sem("out_written")
        stage_done, cleared = sem("stage_done"), sem("cleared")

        def run(engine, which):
            def meet():
                engine.drain().then_inc(stage_done, 1)
                meetings.append(1)
                engine.wait_ge(stage_done, 5 * len(meetings))

            meetings, clears = [], []
            for stage in stages:
                if which == "sync":
                    for s in stage["again"]:
                        engine.sem_clear(s).then_inc(cleared, 1)
                clears.extend(stage["again"])
                if stage["again"]:
                    engine.wait_ge(cleared, len(clears))
                    engine.drain()
                if which in stage:
                    stage[which](engine)
                meet()

        block = ctx.enter_context(nc.Block())

        @block.sync
        def _(sp):
            sp.dma_start(B.h[:, :, :], a["hidden"]).then_inc(start_in, 16)
            sp.dma_start(small[:, 0:5 * C], a["gains"]).then_inc(start_in, 16)
            sp.dma_start(B.ident[:, :], a["ident"]).then_inc(start_in, 16)
            sp.wait_ge(start_in, 48)
            run(sp, "sync")
            sp.dma_start(out, B.x[:, :, NCTX:]).then_inc(out_written, 16)
            sp.wait_ge(out_written, 16)

        @block.tensor
        def _(pe):
            run(pe, "tensor")

        @block.vector
        def _(dve):
            dve.memset(B.ones[:, :], 1.0)
            run(dve, "vector")

        @block.scalar
        def _(act):
            run(act, "scalar")

        @block.gpsimd
        def _(pool):
            run(pool, "gpsimd")


class Arena:

    def __init__(self, ap):
        self.ap, self.at = ap, 0

    def take(self, width, dt=None):
        v = self.ap[:, self.at:self.at + width]
        self.at += width
        return v if dt is None else v.bitcast(dt)



class ModTiles:

    def __init__(self, B, arenas, name, first, per, at):
        self.B, self.first, self.per = B, first, per
        self.w = [ar.take(per * C * P).rearrange("p (m c n) -> p m c n", m=per, c=C) for ar in arenas]
        self.out = at.rearrange("p (m s) -> p m s", s=2)
        self.w_in = [B.sem(f"{name}_w_in{s}") for s in range(2)]
        self.used, self.summed, self.added = (B.sem(f"{name}_{x}") for x in ("w_used", "summed", "added"))

    def load(self, sp, n, slot):
        sp.wait_ge(self.used, n + 1)
        sp.dma_start(self.w[slot].rearrange("p m c n -> p m (c n)"),
                     self.B.a["w_mod"][ds(self.first + n * self.per, self.per)].rearrange("m p c n -> p m (c n)")
                     ).then_inc(self.w_in[slot], 16)

    def multiply(self, pe, n, slot, at):
        pe.wait_ge(self.w_in[slot], 8 * n - 8 * slot + 16)
        for m in range(self.per):
            for c in range(C):
                mm = pe.matmul(self.out[:, at + m, :], self.w[slot][:, m, c, :], self.B.cond[:, c, :],
                               start=c == 0, stop=c == C - 1)
        mm.then_inc(self.used, 1)

    def add(self, dve, n, tiles):
        at = ds(self.first + n * tiles, tiles)
        dve.tensor_tensor(self.B.mod.rearrange("p l k c s -> p (l k c) s")[:, at, :], self.out[:, 0:tiles, :],
                          self.B.mod_bias[:, at].unsqueeze(2).to_broadcast([P, tiles, 2]), ALU.add).then_inc(self.added, 1)


def modulation(B):
    M = 4
    loads = 2 * C // M
    ar = Arena(B.mixer_arena)
    raw = ar.take(C * 2).rearrange("p (c s) -> p c s", s=2)
    tiles = ModTiles(B, (ar, ar), "mod0", 0, M, B.ps[:, 0, 0:4 * C])
    cond_in, cond_ready = B.sem("cond_in"), B.sem("cond_ready")

    def sync(sp):
        sp.dma_start(raw, B.a["cond"]).then_inc(cond_in, 16)
        sp.dma_start(B.mod_bias, B.a["b_mod"]).then_inc(cond_in, 16)
        for n in range(loads):
            tiles.load(sp, n, n % 2)

    def tensor(pe):
        pe.sem_inc(tiles.used, 2)
        pe.wait_ge(cond_ready, 1)
        for n in range(loads):
            tiles.multiply(pe, n, n % 2, n * M)

    def scalar(act):
        act.wait_ge(cond_in, 32)
        act.activation(B.cond, raw, ACT.Silu).then_inc(cond_ready, 1)

    def vector(dve):
        dve.wait_ge(cond_in, 32)
        dve.wait_ge(tiles.used, 2 + loads)
        tiles.add(dve, 0, 2 * C)

    return {"sync": sync, "tensor": tensor, "scalar": scalar, "vector": vector}



def norm(B, layer, gain, shift, scale, segs, split=False):
    dst = B.x
    ar = Arena(B.peer_arena if split else B.mixer_arena)
    t0, n = segs[0][0], sum(s[1] for s in segs)
    sq = [ar.take(T) for _ in range(2)]
    ms, r, tmp = ar.take(T), ar.take(T), ar.take(T)
    factor = ar.take(C * 2).rearrange("p (c s) -> p c s", s=2)
    used, squared, root, chain_s, scaled, shifted, high = (
        B.sem(f"norm_{x}") for x in ("used", "squared", "root", "chain", "scaled", "shifted", "high"))

    def scalar(act):
        for c in range(C):
            act.wait_ge(used, c + 1)
            act.activation(sq[c % 2][:, t0:t0 + n], B.h[:, c, t0:t0 + n], ACT.Square).then_inc(squared, 1)
        act.wait_ge(chain_s, 2 if len(segs) == 1 else 3)
        act.activation(r[:, t0:t0 + n], ms[:, t0:t0 + n], ACT.Sqrt).then_inc(root, 1)
        if shift is not None:
            for c in range(C):
                act.wait_ge(scaled, c + 1)
                for (s0, m, which) in segs:
                    ins = act.activation(dst[:, c, s0:s0 + m], dst[:, c, s0:s0 + m], ACT.Identity,
                                         bias=B.mod[:, layer, shift, c, which:which + 1])
                ins.then_inc(shifted, 1)
                if split:
                    act.wait_ge(shifted, c + 1)
                    act.copy(B.xr[:, 0, c, t0:t0 + n], dst[:, c, t0:t0 + n]).then_inc(high, 1)

    def tensor(pe):
        pe.sem_inc(used, 2)
        for c in range(C):
            pe.wait_ge(squared, c + 1)
            for (s0, m, which) in segs:
                mm = pe.matmul(B.ps[:, which, 0:m], B.ones[:, :], sq[c % 2][:, s0:s0 + m],
                               start=c == 0, stop=c == C - 1)
            mm.then_inc(used, 1)

    def vector(dve):
        chain = Chain(chain_s)
        if shift is not None:
            chain.inc(dve.scalar_tensor_tensor(out=factor, in0=B.mod[:, layer, scale], scalar=1.0,
                                               in1=gain.unsqueeze(2).to_broadcast([P, C, 2]),
                                               op0=ALU.add, op1=ALU.mult))
        else:
            chain.inc(dve.tensor_copy(factor, gain.unsqueeze(2).to_broadcast([P, C, 2])))
        dve.wait_ge(used, C + 2)
        for (s0, m, which) in segs:
            chain.inc(dve.tensor_scalar(ms[:, s0:s0 + m], B.ps[:, which, 0:m], 1.0 / D, EPS, ALU.mult, ALU.add))
        dve.wait_ge(root, 1)
        refined_reciprocal(dve, chain, r[:, t0:t0 + n], ms[:, t0:t0 + n], tmp[:, t0:t0 + n])
        for c in range(C):
            for (s0, m, which) in segs:
                ins = dve.scalar_tensor_tensor(out=dst[:, c, s0:s0 + m], in0=B.h[:, c, s0:s0 + m],
                                               scalar=factor[:, c, which:which + 1], in1=r[:, s0:s0 + m],
                                               op0=ALU.mult, op1=ALU.mult)
            ins.then_inc(scaled, 1)
        if split:
            for c in range(C):
                dve.wait_ge(high, c + 1)
                dve.tensor_tensor(B.xr[:, 1, c, t0:t0 + n], dst[:, c, t0:t0 + n],
                                  B.xr[:, 0, c, t0:t0 + n].bitcast(F32), ALU.subtract)

    def refined_reciprocal(dve, chain, r, ms, tmp):
        chain.wait(dve)
        chain.done(dve, dve.reciprocal(r, r))
        chain.done(dve, dve.tensor_tensor(tmp, r, r, ALU.mult))
        chain.done(dve, dve.tensor_tensor(tmp, tmp, ms, ALU.mult))
        chain.done(dve, dve.tensor_scalar(tmp, tmp, -0.5, 1.5, ALU.mult, ALU.add))
        chain.done(dve, dve.tensor_tensor(r, r, tmp, ALU.mult))

    return {"scalar": scalar, "tensor": tensor, "vector": vector}



def gla(B):
    H, DV2 = GLA_HEADS, GLA_DV // P
    ar = Arena(B.mixer_arena)
    oT = ar.take(C * T).rearrange("p (c t) -> p c t", c=C)
    wqkg = ar.take(C * 512).rearrange("p (c n) -> p c n", c=C)
    wv = ar.take(C * GLA_DV).rearrange("p (c n) -> p c n", c=C)
    wlo = ar.take(C * 2 * GLA_RANK).rearrange("p (c n) -> p c n", c=C)
    lo = ar.take(T)
    walpha = ar.take(2 * 512).rearrange("p (d n) -> p d n", d=2)
    sums = [ar.take((LEVELS + 2) * P) for _ in range(2)]
    masks = ar.take(NMASK * P)
    q, k = ([ar.take(T) for _ in range(2)] for _ in range(2))
    v = [ar.take(CHUNKS * GLA_DV).rearrange("p (n v) -> p n v", n=CHUNKS) for _ in range(2)]
    la = [ar.take(2 * CHUNKS * P) for _ in range(2)]
    dec = ar.take((2 * LEVELS + 2) * P)
    dec_f, dec_b = dec[:, 0:(LEVELS + 2) * P], dec[:, (LEVELS + 2) * P:]
    masked, pT = ar.take(NMASK * P), ar.take(P)
    dec_e = [ar.take(2 * P) for _ in range(2)]
    q_f, k_d, k_t = ar.take(P), ar.take(P), ar.take(P)
    q_b = ar.take(T)
    s_f = [ar.take(GLA_DV) for _ in range(2)]
    s_b = ar.take(CHUNKS * GLA_DV).rearrange("p (n v) -> p n v", n=CHUNKS)
    o = ar.take(DV2 * T).rearrange("p (v t) -> p v t", v=DV2)
    sq = masked[:, 0:DV2 * T].rearrange("p (v t) -> p v t", v=DV2)
    ms, r, tmp = dec[:, 0:T], dec[:, T:2 * T], masked[:, 0:T]
    ngain = ar.take(DV2)
    LOW = 2 * GLA_RANK + 1
    ps = B.ps
    MOD = 4 * C // H
    BESIDE = [range(MOD * s // CHUNKS, MOD * (s + 1) // CHUNKS) for s in range(CHUNKS)]
    mod = ModTiles(B, (ar, ar), "mod1", 2 * C, 1, ps[:, 7, 0:2 * MOD])

    names = ("const_in", "w_in", "wv_in", "lo_mm", "lo_ev", "u_mm", "u_ev", "z_chain", "z_act", "la_ok", "passed",
             "eb_mm", "eb_ok", "kd_ok", "kt_mm", "kt_ok", "st_mm", "st_ok",
             "ex_mm", "ex_ok", "rf_ok", "rb_ok", "sc_mm", "sc_read", "pt_ok", "fkt_mm", "fkt_ok", "fst_mm", "fst_ok",
             "o_mm", "o_ev", "sq_ok", "ms_mm", "ms_ok", "root_ok", "silu_ok", "head_ok", "dve_chain")
    (const_in, w_in, wv_in, lo_mm, lo_ev, u_mm, u_ev, z_chain, z_act, la_ok, passed,
     eb_mm, eb_ok, kd_ok, kt_mm, kt_ok, st_mm, st_ok,
     ex_mm, ex_ok, rf_ok, rb_ok, sc_mm, sc_read, pt_ok, fkt_mm, fkt_ok, fst_mm, fst_ok,
     o_mm, o_ev, sq_ok, ms_mm, ms_ok, root_ok, silu_ok, head_ok, dve_chain) = (B.sem("gla_" + x) for x in names)
    NB = len(BACKWARD) - 1
    scale = P ** -0.5
    Q, K, G0, G1, V, Z = range(6)

    UNITS = [(K, CTX), (Z, (1, 0)), (Q, CTX), (Z, (1, 1)), (G0, CTX), (Z, (0, 0)), (G1, CTX), (Z, (0, 1)),
             (K, LAT), (Q, LAT), (G0, LAT), (G1, LAT), (V, 0), (V, 1), (V, 2)]
    NU = len(UNITS)
    NZ = sum(what == Z for what, _ in UNITS)
    NP = NU - NZ
    LAST_QKG = max(u for u, (what, _) in enumerate(UNITS) if what < V)
    QK_DONE = 1 + max(n for n, (what, _) in enumerate(x for x in UNITS if x[0] != Z) if what in (Q, K))
    IN_BACKWARD = [(0, 1), (2, 3), (4, 5), (6, 7), (8,), ()]
    IN_FORWARD = [9, 10, 11, 12, 13, 14]

    def place(h, u):
        kind = UNITS[u][0] == Z
        return (NZ if kind else NP) * h + sum((what == Z) == kind for what, _ in UNITS[:u + 1])

    def unit_bank(par, u):
        return (4, 6)[(NU * par + u) % 2]

    def half_chunks(part):
        d, j = part
        return slice((d * CHUNKS + j * 3) * P, (d * CHUNKS + j * 3 + 3) * P)

    def heads(engine, head):
        head(0, 0, True, False)
        with engine.Fori(0, (H - 2) // 2) as i:
            head(2 * i + 1, 1, False, False)
            head(2 * i + 2, 0, False, False)
        head(H - 1, 1, False, True)

    def block(ap, level, half):
        return ap.rearrange("p (n two w) -> p n two w", two=2, w=1 << level)[:, :, half, :]

    def sync(sp):
        def weights(h):
            sp.dma_start(wqkg, B.a["gla_w_qkg"][ds(h, 1)].squeeze(0)).then_inc(w_in, 16)

        def v_weights(h):
            sp.dma_start(wv, B.a["gla_w_v"][ds(h, 1)].squeeze(0)).then_inc(wv_in, 16)

        def next_weights(h):
            sp.wait_ge(u_mm, NU * h - NU + LAST_QKG + 1)
            weights(h)
            sp.wait_ge(u_mm, NU * h)
            v_weights(h)

        sp.dma_start(wlo, B.a["gla_w_lo"]).then_inc(const_in, 16)
        sp.dma_start(lo[LOW - 1:LOW], B.a["ones_row"]).then_inc(const_in, 16)
        sp.dma_start(walpha[0:LOW], B.a["gla_w_alpha"]).then_inc(const_in, 16)
        weights(0)
        v_weights(0)
        sp.dma_start(sums[0], B.a["range_sums"][0]).then_inc(const_in, 16)
        sp.dma_start(sums[1], B.a["range_sums"][1]).then_inc(const_in, 16)
        sp.dma_start(masks, B.a["gla_masks"]).then_inc(const_in, 16)
        sp.dma_start(ngain, B.a["gla_norm_g"]).then_inc(const_in, 16)
        next_weights(1)
        with sp.Fori(0, H - 2) as h:
            for m in range(MOD):
                mod.load(sp, MOD * h + m, m % 2)
            next_weights(h + 2)
        with sp.Fori(0, 2) as i:
            for m in range(MOD):
                mod.load(sp, MOD * (H - 2) + MOD * i + m, m % 2)

    def tensor(pe):
        def products(h, what, part, bank):
            if what == Z:
                d, j = part
                return [(ps[:, bank, n * P:n * P + P], lo[0:LOW, (3 * j + n) * P:(3 * j + n + 1) * P],
                         walpha[0:LOW, d, ds(h * P, P)], True, True) for n in range(3)]
            if what == V:
                return [(ps[:, bank, n * GLA_DV:n * GLA_DV + GLA_DV], B.x[:, c, (2 * part + n) * P:(2 * part + n + 1) * P],
                         wv[:, c, :], c == 0, c == C - 1) for n in range(2) for c in range(C)]
            s0, m, _ = part
            return [(ps[:, bank, 0:m], wqkg[:, c, what * P:what * P + P], B.x[:, c, s0:s0 + m], c == 0, c == C - 1)
                    for c in range(C)]

        def unit(h, par, u, pieces=(0, 1)):
            what, part = UNITS[u]
            todo = products(h, what, part, unit_bank(par, u))
            cut = len(todo) * 5 // 8
            if 0 in pieces:
                if u >= 2:
                    pe.wait_ge(la_ok if UNITS[u - 2][0] == Z else u_ev, place(h, u - 2))
                elif not isinstance(h, int) or h > 0:
                    pe.wait_ge(la_ok if UNITS[NU - 2 + u][0] == Z else u_ev, place(h - 1, NU - 2 + u))
                if what != Z:
                    pe.wait_ge(wv_in if what == V else w_in, 16 * h + 16)
                for out, left, right, start, stop in todo[:cut]:
                    pe.matmul(out, left, right, start=start, stop=stop)
            if 1 in pieces:
                for out, left, right, start, stop in todo[cut:]:
                    mm = pe.matmul(out, left, right, start=start, stop=stop)
                mm.then_inc(u_mm, 1)

        def mean_square(h):
            pe.wait_ge(sq_ok, h + 1)
            for n, (s0, m, _) in enumerate((CTX, LAT)):
                for v2 in range(DV2):
                    mm = pe.matmul(ps[:, 2 + n, 0:m], B.ones[:, :], sq[:, v2, s0:s0 + m], start=v2 == 0, stop=v2 == DV2 - 1)
            mm.then_inc(ms_mm, 1)

        def head(h, par, first, last):
            def edge_sums(s):
                c = BACKWARD[s]
                pe.matmul(ps[:, s % 2, 0:2 * P], la[par][:, (CHUNKS + c) * P:(CHUNKS + c + 1) * P],
                          sums[1][:, LEVELS * P:], start=True, stop=True).then_inc(eb_mm, 1)

            def level_sums(c):
                left, right = la[par][:, c * P:c * P + P], la[par][:, (CHUNKS + c) * P:(CHUNKS + c + 1) * P]
                pe.matmul(ps[:, 0, :], left, sums[0][:, 0:512], start=True, stop=True)
                pe.matmul(ps[:, 1, :], left, sums[0][:, 512:1024], start=True, stop=True)
                pe.matmul(ps[:, 2, 0:P], left, sums[0][:, 1024:1152], start=True, stop=True)
                pe.matmul(ps[:, 2, P:512], right, sums[1][:, 0:384], start=True, stop=True)
                pe.matmul(ps[:, 3, :], right, sums[1][:, 384:896], start=True, stop=True).then_inc(ex_mm, 1)

            pe.wait_ge(la_ok, NZ * h + NZ)
            edge_sums(0)
            for s in range(CHUNKS):
                c = BACKWARD[s]
                if s < NB:
                    edge_sums(s + 1)
                if not last:
                    for u in IN_BACKWARD[s]:
                        unit(h + 1, 1 - par, u)
                if s == 0:
                    pe.wait_ge(u_ev, NP * h + NP)
                    if not first:
                        pe.wait_ge(o_ev, CHUNKS * h)
                        mean_square(h - 1)
                if s < NB:
                    pe.wait_ge(kd_ok, NB * h + s + 1)
                    pe.transpose(ps[:, 5, 0:P], k_d, B.ident[:, :]).then_inc(kt_mm, 1)
                for m in BESIDE[s]:
                    mod.multiply(pe, MOD * h + m, m % 2, m)
                if s < NB:
                    pe.wait_ge(kt_ok, NB * h + s + 1)
                    pe.matmul(ps[:, 5, P:P + GLA_DV], k_t, v[par][:, c, :], start=True, stop=True).then_inc(st_mm, 1)
            pe.wait_ge(st_ok, NB * h + NB)
            pe.wait_ge(eb_ok, CHUNKS * h + CHUNKS)
            if not first:
                pe.wait_ge(ms_ok, h)
            level_sums(0)
            pe.wait_ge(mod.added, h + 1)
            for c in FORWARD:
                if not last:
                    unit(h + 1, 1 - par, IN_FORWARD[c], (0,))
                pe.wait_ge(rf_ok, CHUNKS * h + c + 1)
                pe.wait_ge(ex_ok, 2 * CHUNKS * h + 2 * c + 2)
                pe.matmul(ps[:, 3, 2 * P:3 * P], k[par][:, c * P:c * P + P], q[par][:, c * P:c * P + P],
                          start=True, stop=True)
                if c < CHUNKS - 1:
                    pe.transpose(ps[:, 5, 0:P], k_d, B.ident[:, :]).then_inc(fkt_mm, 1)
                for n in range(2 * LEVELS):
                    if n == LEVELS:
                        pe.wait_ge(rb_ok, CHUNKS * h + c + 1)
                    at = n if n < LEVELS else n + 2
                    both = dec[:, at * P:at * P + P]
                    mm = pe.matmul(ps[:, n // 4, n % 4 * P:n % 4 * P + P], both, both, start=True, stop=True)
                mm.then_inc(sc_mm, 1)
                if c < CHUNKS - 1:
                    pe.wait_ge(fkt_ok, (CHUNKS - 1) * h + c + 1)
                    pe.matmul(ps[:, 5, P:P + GLA_DV], k_t, v[par][:, c, :], start=True, stop=True).then_inc(fst_mm, 1)
                if not last:
                    unit(h + 1, 1 - par, IN_FORWARD[c], (1,))
                if c < CHUNKS - 1:
                    pe.wait_ge(sc_read, CHUNKS * h + c + 1)
                    level_sums(c + 1)
                pe.wait_ge(pt_ok, CHUNKS * h + c + 1)
                if c:
                    pe.wait_ge(fst_ok, (CHUNKS - 1) * h + c)
                    pe.wait_ge(o_ev, CHUNKS * h + c)
                for n in range(DV2):
                    half = slice(n * P, n * P + P)
                    more = [(v[par][:, c, half], pT)]
                    if c:
                        more.append((s_f[c % 2][:, half], q_f))
                    if c != BACKWARD[0]:
                        more.append((s_b[:, c, half], q_b[:, c * P:c * P + P]))
                    for m, (left, right) in enumerate(more):
                        mm = pe.matmul(ps[:, 7, half], left, right, start=m == 0, stop=m == len(more) - 1)
                mm.then_inc(o_mm, 1)

        pe.wait_ge(const_in, 7 * 16)
        for n, (s0, m, _) in enumerate((CTX, LAT)):
            for c in range(C):
                mm = pe.matmul(ps[0:LOW - 1, n, 0:m], wlo[:, c, :], B.x[:, c, s0:s0 + m], start=c == 0, stop=c == C - 1)
        mm.then_inc(lo_mm, 1)
        pe.sem_inc(mod.used, 2)
        pe.wait_ge(lo_ev, 1)
        for u in range(NU):
            unit(0, 0, u)
        heads(pe, head)
        mean_square(H - 1)

    def scalar(act):
        def unit(h, par, u):
            what, part = UNITS[u]
            bank = unit_bank(par, u)
            act.wait_ge(u_mm, NU * h + u + 1)
            if what == Z:
                to = la[par][:, half_chunks(part)]
                n = place(h, u) * 2
                act.activation(to, ps[:, bank, 0:3 * P], ACT.Abs).then_inc(z_chain, 1)
                act.wait_ge(z_chain, n - 1)
                act.activation(to, to, ACT.Exp, scale=-1.0).then_inc(z_chain, 1)
                act.wait_ge(z_chain, n)
                act.activation(to, to, ACT.Ln, bias=1.0).then_inc(z_act, 1)
            elif what == V:
                act.copy(v[par][:, 2 * part:2 * part + 2, :].rearrange("p n v -> p (n v)"), ps[:, bank, :]).then_inc(u_ev, 1)
            elif what in (Q, K):
                s0, m, _ = part
                act.mul((q, k)[what][par][:, s0:s0 + m], ps[:, bank, 0:m], scale if what == Q else 1.0).then_inc(u_ev, 1)
            else:
                s0, m, _ = part
                act.sem_inc(passed, 1)
                act.copy(oT[:, ds(DV2 * h + what - G0, 1), s0:s0 + m].squeeze(1), ps[:, bank, 0:m]).then_inc(u_ev, 1)

        def root(h):
            act.wait_ge(ms_ok, h + 1)
            act.activation(r, ms, ACT.Sqrt).then_inc(root_ok, 1)

        def silu(h):
            act.wait_ge(u_ev, NP * h + NP)
            act.sem_inc(passed, 1)
            g = oT[:, ds(DV2 * h, DV2), :]
            act.activation(g, g, ACT.Silu).then_inc(silu_ok, 1)

        def head(h, par, first, last):
            def edge_decays(s):
                act.wait_ge(eb_mm, CHUNKS * h + s + 1)
                if s >= 2:
                    act.wait_ge(st_ok, NB * h + s - 1)
                act.activation(dec_e[s % 2], ps[:, s % 2, 0:2 * P], ACT.Exp, scale=1.0 / GLA_TAU).then_inc(eb_ok, 1)

            def level_decays(c):
                act.wait_ge(ex_mm, CHUNKS * h + c + 1)
                if c:
                    act.wait_ge(fst_ok, (CHUNKS - 1) * h + c)
                elif not first:
                    act.wait_ge(head_ok, h)
                flat = ps[:, 0:4, :].rearrange("p b n -> p (b n)")
                cut = (LEVELS + 2) * P
                act.activation(dec_f, flat[:, 0:cut], ACT.Exp, scale=1.0 / GLA_TAU).then_inc(ex_ok, 1)
                act.activation(dec_b, flat[:, cut:], ACT.Exp, scale=1.0 / GLA_TAU).then_inc(ex_ok, 1)

            edge_decays(0)
            for s in range(CHUNKS):
                if s < NB:
                    edge_decays(s + 1)
                    act.wait_ge(kt_mm, NB * h + s + 1)
                    act.copy(k_t, ps[:, 5, 0:P]).then_inc(kt_ok, 1)
                if not last:
                    for u in IN_BACKWARD[s]:
                        unit(h + 1, 1 - par, u)
                if not first and s == 0:
                    root(h - 1)
                if not first and s == 1:
                    silu(h - 1)
            level_decays(0)
            for c in FORWARD:
                if c < CHUNKS - 1:
                    act.wait_ge(fkt_mm, (CHUNKS - 1) * h + c + 1)
                    act.copy(k_t, ps[:, 5, 0:P]).then_inc(fkt_ok, 1)
                if not last:
                    unit(h + 1, 1 - par, IN_FORWARD[c])
                if c < CHUNKS - 1:
                    level_decays(c + 1)
                act.wait_ge(o_mm, CHUNKS * h + c + 1)
                act.copy(o[:, :, c * P:c * P + P], ps[:, 7, 0:GLA_DV].rearrange("p (v t) -> p v t", v=DV2)).then_inc(o_ev, 1)
            act.wait_ge(o_ev, CHUNKS * h + CHUNKS)
            act.activation(sq, o, ACT.Square).then_inc(sq_ok, 1)

        act.wait_ge(lo_mm, 1)
        for n, (s0, m, _) in enumerate((CTX, LAT)):
            ins = act.copy(lo[0:LOW - 1, s0:s0 + m], ps[0:LOW - 1, n, 0:m])
        ins.then_inc(lo_ev, 1)
        for u in range(NU):
            unit(0, 0, u)
        heads(act, head)
        silu(H - 1)
        root(H - 1)

    def vector(dve):
        chain = Chain(dve_chain)

        def log_gates(h, par, u):
            dve.wait_ge(z_act, place(h, u))
            to = la[par][:, half_chunks(UNITS[u][1])]
            dve.scalar_tensor_tensor(out=to, in0=ps[:, unit_bank(par, u), 0:3 * P], scalar=0.0, in1=to,
                                     op0=ALU.min, op1=ALU.subtract).then_inc(la_ok, 1)

        def finish(h):
            chain.loop(h, 7)
            dve.wait_ge(ms_mm, h + 1)
            dve.tensor_scalar(ms[:, 0:NCTX], ps[:, 2, 0:NCTX], 1.0 / GLA_DV, EPS, ALU.mult, ALU.add)
            dve.tensor_scalar(ms[:, NCTX:], ps[:, 3, :], 1.0 / GLA_DV, EPS, ALU.mult, ALU.add).then_inc(ms_ok, 1)
            yield
            dve.wait_ge(root_ok, h + 1)
            chain.done(dve, dve.reciprocal(r, r))
            yield
            chain.done(dve, dve.tensor_tensor(tmp, r, r, ALU.mult))
            chain.done(dve, dve.tensor_tensor(tmp, tmp, ms, ALU.mult))
            yield
            chain.done(dve, dve.tensor_scalar(tmp, tmp, -0.5, 1.5, ALU.mult, ALU.add))
            chain.done(dve, dve.tensor_tensor(r, r, tmp, ALU.mult))
            yield
            for n in range(DV2):
                chain.inc(dve.scalar_tensor_tensor(out=o[:, n, :], in0=o[:, n, :], scalar=ngain[:, n:n + 1], in1=r,
                                                   op0=ALU.mult, op1=ALU.mult))
            chain.wait(dve)
            yield
            dve.wait_ge(silu_ok, h + 1)
            g = oT[:, ds(DV2 * h, DV2), :]
            dve.tensor_tensor(g, o, g, ALU.mult).then_inc(head_ok, 1)
            assert chain.n == chain.per
            chain.n = 0

        def head(h, par, first, last):
            beside = iter(()) if first else finish(h - 1)
            dve.wait_ge(u_ev, NP * h + QK_DONE)
            if not first:
                dve.wait_ge(o_mm, CHUNKS * h)
            for s, c in enumerate(BACKWARD):
                e = dec_e[s % 2]
                dve.wait_ge(eb_ok, CHUNKS * h + s + 1)
                dve.tensor_tensor(q_b[:, c * P:c * P + P], q[par][:, c * P:c * P + P], e[:, 0:P], ALU.mult)
                if s < NB:
                    if s:
                        dve.wait_ge(kt_mm, NB * h + s)
                    dve.tensor_tensor(k_d, k[par][:, c * P:c * P + P], e[:, P:2 * P], ALU.mult).then_inc(kd_ok, 1)
                next(beside, None)
                if s < NB:
                    dve.wait_ge(st_mm, NB * h + s + 1)
                    to = s_b[:, BACKWARD[s + 1], :]
                    if s == 0:
                        dve.tensor_copy(to, ps[:, 5, P:P + GLA_DV]).then_inc(st_ok, 1)
                    else:
                        dve.wait_ge(st_ok, NB * h + s)
                        dve.scalar_tensor_tensor(out=to, in0=s_b[:, c, :], scalar=e[:, 0:1],
                                                 in1=ps[:, 5, P:P + GLA_DV], op0=ALU.mult, op1=ALU.add).then_inc(st_ok, 1)
                if not last:
                    for u in IN_BACKWARD[s]:
                        if UNITS[u][0] == Z:
                            log_gates(h + 1, 1 - par, u)
            for _ in beside:
                pass
            dve.wait_ge(mod.used, MOD * h + MOD + 2)
            mod.add(dve, h, MOD)
            for c in FORWARD:
                here = slice(c * P, c * P + P)
                dve.wait_ge(ex_ok, 2 * CHUNKS * h + 2 * c + 1)
                if c:
                    dve.wait_ge(sc_mm, CHUNKS * h + c)
                dve.tensor_tensor(k_d, k[par][:, here], dec_f[:, TO_END * P:TO_END * P + P], ALU.mult)
                for n in range(LEVELS):
                    at = dec_f[:, n * P:n * P + P]
                    dve.tensor_tensor(block(at, n, 0), block(k[par][:, here], n, 0), block(at, n, 0), ALU.mult)
                    dve.tensor_tensor(block(at, n, 1), block(q[par][:, here], n, 1), block(at, n, 1), ALU.mult)
                if c:
                    dve.wait_ge(o_mm, CHUNKS * h + c)
                dve.tensor_tensor(q_f, q[par][:, here], dec_f[:, TO_START * P:TO_START * P + P], ALU.mult).then_inc(rf_ok, 1)
                dve.wait_ge(sc_mm, CHUNKS * h + c + 1)
                dve.tensor_tensor(masked, ps[:, 0:4, :].rearrange("p b n -> p (b n)")[:, 0:NMASK * P],
                                  masks, ALU.mult).then_inc(sc_read, 1)
                if c < CHUNKS - 1:
                    dve.wait_ge(fst_mm, (CHUNKS - 1) * h + c + 1)
                    to = s_f[(c + 1) % 2]
                    if c == 0:
                        dve.tensor_copy(to, ps[:, 5, P:P + GLA_DV]).then_inc(fst_ok, 1)
                    else:
                        dve.wait_ge(fst_ok, (CHUNKS - 1) * h + c)
                        dve.scalar_tensor_tensor(out=to, in0=s_f[c % 2], scalar=dec_f[:, TO_START * P + P - 1:TO_START * P + P],
                                                 in1=ps[:, 5, P:P + GLA_DV], op0=ALU.mult, op1=ALU.add).then_inc(fst_ok, 1)
                dve.wait_ge(sc_read, CHUNKS * h + c + 1)
                dve.tensor_reduce(pT, masked.rearrange("p (n i) -> p i n", n=NMASK), AX.X, ALU.add).then_inc(pt_ok, 1)

        dve.wait_ge(const_in, 7 * 16)
        for u in range(NU):
            if UNITS[u][0] == Z:
                log_gates(0, 0, u)
        heads(dve, head)
        for _ in finish(H - 1):
            pass

    def gpsimd(pool):
        def head(h, par, first, last):
            pool.wait_ge(u_ev, NP * h + QK_DONE)
            for c in FORWARD:
                here = slice(c * P, c * P + P)
                pool.wait_ge(ex_ok, 2 * CHUNKS * h + 2 * c + 2)
                for n in range(LEVELS):
                    at = dec_b[:, n * P:n * P + P]
                    pool.tensor_tensor(block(at, n, 0), block(q[par][:, here], n, 0), block(at, n, 0), ALU.mult)
                    ins = pool.tensor_tensor(block(at, n, 1), block(k[par][:, here], n, 1), block(at, n, 1), ALU.mult)
                ins.then_inc(rb_ok, 1)

        heads(pool, head)

    return {"sync": sync, "tensor": tensor, "scalar": scalar, "vector": vector, "gpsimd": gpsimd}



def project_out(B, w_dram, t_first, layer, segs):
    ar = Arena(B.mixer_arena)
    mixed = ar.take(C * T).rearrange("p (c t) -> p c t", c=C)
    w = [ar.take(C * P).rearrange("p (c n) -> p c n", c=C) for _ in range(2)]
    w_in = [B.sem(f"out_w_in{s}") for s in range(2)]
    w_used, summed, added = (B.sem(f"out_{x}") for x in ("w_used", "summed", "added"))

    def sync(sp):
        with sp.Fori(0, C // 2) as i:
            for s in range(2):
                sp.wait_ge(w_used, 2 * i + s + 1)
                sp.dma_start(w[s], w_dram[ds(2 * i + s, 1)].squeeze(0)).then_inc(w_in[s], 16)

    def tensor(pe):
        pe.sem_inc(w_used, 2)
        with pe.Fori(0, C // 2) as i:
            for s in range(2):
                pe.wait_ge(w_in[s], 16 * i + 16)
                pe.wait_ge(added, 2 * i + s + 1)
                for (s0, m, which) in segs:
                    for c in range(C):
                        mm = pe.matmul(B.ps[:, 2 * s + which, 0:m], w[s][:, c, :],
                                       mixed[:, c, s0 - t_first:s0 - t_first + m], start=c == 0, stop=c == C - 1)
                mm.then_inc(summed, 1)
                pe.wait_ge(summed, 2 * i + s + 1)
                pe.sem_inc(w_used, 1)

    def vector(dve):
        dve.sem_inc(added, 2)
        with dve.Fori(0, C // 2) as i:
            for s in range(2):
                dve.wait_ge(summed, 2 * i + s + 1)
                for (s0, m, which) in segs:
                    h = B.h[:, ds(2 * i + s, 1), s0:s0 + m]
                    ins = dve.scalar_tensor_tensor(out=h, in0=B.ps[:, 2 * s + which:2 * s + which + 1, 0:m],
                                                   scalar=B.mod[:, layer, 2, ds(2 * i + s, 1), which],
                                                   in1=h, op0=ALU.mult, op1=ALU.add)
                ins.then_inc(added, 1)

    return {"sync": sync, "tensor": tensor, "vector": vector}



def attention(B):
    H, QT, KT = DIFF_HEADS, NLAT // P, T // P
    ar = Arena(B.mixer_arena)
    mixed = ar.take(C * T).rearrange("p (c t) -> p c t", c=C)
    w = [ar.take(C * 3 * P).rearrange("p (c n) -> p c n", c=C) for _ in range(2)]
    cos, sin, swap = ar.take(NLAT), ar.take(NLAT), ar.take(P)
    raw, turned = ([ar.take(NLAT) for _ in range(2)] for _ in range(2))
    q, k = ([ar.take(n) for _ in range(2)] for n in (NLAT, T))
    v = [ar.take(T).rearrange("p (n v) -> p n v", n=KT) for _ in range(2)]
    p = [[ar.take(T) for _ in range(2)] for _ in range(2)]
    aT = ar.take(KT * NLAT).rearrange("p (n t) -> p n t", n=KT)
    o, sq, ms, r, tmp = (ar.take(NLAT) for _ in range(5))
    stat = [[ar.take(8) for _ in range(2)] for _ in range(2)]
    lam_in, lam, ngain = ar.take(4 * HD), ar.take(8), ar.take(1)
    ps = B.ps
    names = ("const_in", "w_in0", "w_in1", "u_mm", "u_ev", "turn_mm", "turn_read", "cos_chain", "qk_ok", "s_mm", "max_ok",
             "exp_ok", "p_ok", "at_mm", "at_ev", "o_mm", "o_ev", "o_used", "sq_ok", "ms_mm", "ms_ok", "root_ok",
             "lam_a", "lam_b", "lam_chain", "soft_chain", "finish_chain")
    (const_in, w_in0, w_in1, u_mm, u_ev, turn_mm, turn_read, cos_chain, qk_ok, s_mm, max_ok,
     exp_ok, p_ok, at_mm, at_ev, o_mm, o_ev, o_used, sq_ok, ms_mm, ms_ok, root_ok,
     lam_a, lam_b, lam_chain, soft_chain, finish_chain) = (B.sem("att_" + x) for x in names)
    w_in = (w_in0, w_in1)

    Q, KL, V0, KC, V1, TURN_Q, TURN_K = range(7)
    BANK = (7, 6, 7, 6, 6, 7, 6)
    NP = 5
    FIRST_HALF = [(Q,), (KL,), (V0,), (KC,)]
    SECOND_HALF = [(), (TURN_Q,), (TURN_K,), ()]
    AT_END = (V1,)

    def heads(engine, head):
        head(0, 0, True, False)
        with engine.Fori(0, (H - 2) // 2) as i:
            head(2 * i + 1, 1, False, False)
            head(2 * i + 2, 0, False, False)
        head(H - 1, 1, False, True)

    def prologue(unit):
        for u in (Q, KL, TURN_Q, V0, TURN_K, KC, V1):
            unit(0, 0, u)

    def sync(sp):
        def weights(n, slot):
            sp.dma_start(w[slot], B.a["diff_w_in"][ds(n, 1)].squeeze(0)).then_inc(w_in[slot], 16)

        weights(0, 0)
        for to, name in ((cos, "cos"), (sin, "sin"), (swap, "swap"), (lam_in, "diff_lambda"), (ngain, "diff_norm_g")):
            sp.dma_start(to, B.a[name]).then_inc(const_in, 16)
        weights(1, 1)
        with sp.Fori(0, H // 2 - 1) as i:
            for slot in range(2):
                sp.wait_ge(u_mm, NP * (2 * i + slot) + NP)
                weights(2 * i + slot + 2, slot)

    def tensor(pe):
        def unit(n, par, u):
            bank = BANK[u]
            if u in (Q, KL) and not (isinstance(n, int) and n == 0):
                if isinstance(n, int) and n == 1:
                    pe.wait_ge(u_ev, NP)
                elif u == Q:
                    pe.wait_ge(o_ev, n - 1)
                else:
                    pe.wait_ge(ms_ok, n - 1)
            if u in (TURN_Q, TURN_K):
                z = u - TURN_Q
                pe.wait_ge(u_ev, NP * n + z + 1)
                pe.matmul(ps[:, bank, :], swap, raw[z], start=True, stop=True).then_inc(turn_mm, 1)
                return
            if u == V0:
                pe.wait_ge(turn_read, 2 * n + 1)
            if u == KC:
                pe.wait_ge(turn_read, 2 * n + 2)
            if u == V1:
                pe.wait_ge(u_ev, NP * n + KC + 1)
            pe.wait_ge(w_in[par], 8 * n - 8 * par + 16)
            if u in (V0, V1):
                for t in range(4) if u == V0 else range(4, KT):
                    for c in range(C):
                        mm = pe.matmul(ps[:, bank, t % 4 * P:t % 4 * P + P], B.x[:, c, t * P:t * P + P],
                                       w[par][:, c, 2 * P:3 * P], start=c == 0, stop=c == C - 1)
            else:
                col, s0, m = {Q: (0, NCTX, NLAT), KL: (P, NCTX, NLAT), KC: (P, 0, NCTX)}[u]
                for c in range(C):
                    mm = pe.matmul(ps[:, bank, 0:m], w[par][:, c, col:col + P], B.x[:, c, s0:s0 + m],
                                   start=c == 0, stop=c == C - 1)
            mm.then_inc(u_mm, 1)

        def mean_square(h):
            pe.wait_ge(sq_ok, h + 1)
            pe.matmul(ps[:, 6, :], B.ones[:, :], sq, start=True, stop=True).then_inc(ms_mm, 1)

        def head(h, par, first, last):
            def scores(t):
                for m in range(2):
                    for n in range(2):
                        mm = pe.matmul(ps[:, 2 * m + n, 0:384], q[par][m * HD:m * HD + HD, t * P:t * P + P],
                                       k[par][m * HD:m * HD + HD, n * 384:n * 384 + 384], start=True, stop=True)
                    mm.then_inc(s_mm, 1)

            pe.wait_ge(qk_ok, 2 * h + 2)
            pe.wait_ge(u_ev, NP * h + NP)
            if not first:
                pe.wait_ge(exp_ok, 2 * QT * h)
            scores(0)
            if not first:
                mean_square(h - 1)
            for t in range(QT):
                if not last:
                    for u in FIRST_HALF[t]:
                        unit(h + 1, 1 - par, u)
                if t + 1 < QT:
                    pe.wait_ge(exp_ok, 2 * QT * h + 2 * t + 2)
                    scores(t + 1)
                if not last:
                    for u in SECOND_HALF[t]:
                        unit(h + 1, 1 - par, u)
                pe.wait_ge(p_ok, QT * h + t + 1)
                if t or not first:
                    pe.wait_ge(at_ev, QT * h + t)
                for n in range(KT):
                    mm = pe.transpose(ps[:, 4 + n // 4, n % 4 * P:n % 4 * P + P], p[t % 2][0][:, n * P:n * P + P],
                                      B.ident[:, :])
                mm.then_inc(at_mm, 1)
            if not last:
                for u in AT_END:
                    unit(h + 1, 1 - par, u)
            pe.wait_ge(at_ev, QT * h + QT)
            if last:
                pe.wait_ge(o_ev, h)
                pe.wait_ge(ms_ok, h)
            else:
                pe.wait_ge(u_ev, NP * h + NP + NP)
            for n in range(KT):
                mm = pe.matmul(ps[:, 7, :], v[par][:, n, :], aT[:, n, :], start=n == 0, stop=n == KT - 1)
            mm.then_inc(o_mm, 1)

        pe.wait_ge(const_in, 5 * 16)
        prologue(unit)
        heads(pe, head)
        mean_square(H - 1)

    def scalar(act):
        def unit(n, par, u):
            if u in (TURN_Q, TURN_K):
                return
            act.wait_ge(u_mm, NP * n + u + 1)
            if u == Q and not (isinstance(n, int) and n == 0):
                act.wait_ge(qk_ok, 2 * n)
            to = {Q: raw[0], KL: raw[1], KC: k[par][:, 0:NCTX], V0: v[par][:, 0:4, :].rearrange("p n v -> p (n v)"),
                  V1: v[par][:, 4:6, :].rearrange("p n v -> p (n v)")}[u]
            act.copy(to, ps[:, BANK[u], 0:NLAT if u in (Q, KL, V0) else NCTX]).then_inc(u_ev, 1)

        def root(h):
            act.wait_ge(ms_ok, h + 1)
            act.activation(r, ms, ACT.Sqrt).then_inc(root_ok, 1)

        def head(h, par, first, last):
            def exps(t):
                if t >= 2 or not first:
                    act.wait_ge(at_mm, QT * h + t - 1)
                for m in range(2):
                    act.wait_ge(max_ok, 2 * QT * h + 2 * t + m + 1)
                    act.activation(p[t % 2][m].rearrange("p (n k) -> p n k", n=2), ps[:, 2 * m:2 * m + 2, 0:384], ACT.Exp,
                                   bias=stat[t % 2][m][:, 1:2], scale=HD ** -0.5,
                                   accum_out=stat[t % 2][m][:, 2:3]).then_inc(exp_ok, 1)

            exps(0)
            if not first:
                root(h - 1)
            for t in range(QT):
                if not last:
                    for u in FIRST_HALF[t]:
                        unit(h + 1, 1 - par, u)
                if t + 1 < QT:
                    exps(t + 1)
                if not last:
                    for u in SECOND_HALF[t]:
                        unit(h + 1, 1 - par, u)
                act.wait_ge(at_mm, QT * h + t + 1)
                act.copy(aT[:, 0:4, t * P:t * P + P], ps[:, 4, :].rearrange("p (n k) -> p n k", n=4))
                act.copy(aT[:, 4:6, t * P:t * P + P], ps[:, 5, 0:2 * P].rearrange("p (n k) -> p n k", n=2)).then_inc(at_ev, 1)
            if not last:
                for u in AT_END:
                    unit(h + 1, 1 - par, u)
            act.wait_ge(o_mm, h + 1)
            if not first:
                act.wait_ge(o_used, h)
            act.copy(o, ps[:, 7, :]).then_inc(o_ev, 1)
            act.wait_ge(o_ev, h + 1)
            act.activation(sq, o, ACT.Square).then_inc(sq_ok, 1)

        act.wait_ge(lam_a, 1)
        act.activation(lam[:, 2:4], lam[:, 0:2], ACT.Exp).then_inc(lam_b, 1)
        prologue(unit)
        heads(act, head)
        root(H - 1)

    def vector(dve):
        soft, fin, lam_steps = Chain(soft_chain), Chain(finish_chain), Chain(lam_chain)

        def unit(n, par, u):
            if u not in (TURN_Q, TURN_K):
                return
            z = u - TURN_Q
            dve.wait_ge(turn_mm, 2 * n + z + 1)
            dve.tensor_tensor(turned[z], ps[:, BANK[u], :], sin, ALU.mult).then_inc(turn_read, 1)
            dve.tensor_tensor(raw[z], raw[z], cos, ALU.mult).then_inc(cos_chain, 1)
            dve.wait_ge(turn_read, 2 * n + z + 1)
            dve.wait_ge(cos_chain, 2 * n + z + 1)
            to = q[par] if z == 0 else k[par][:, NCTX:]
            dve.tensor_tensor(to, raw[z], turned[z], ALU.add).then_inc(qk_ok, 1)

        def finish(h):
            fin.loop(h, 5)
            dve.wait_ge(ms_mm, h + 1)
            dve.tensor_scalar(ms, ps[:, 6, :], 1.0 / (2 * HD), EPS, ALU.mult, ALU.add).then_inc(ms_ok, 1)
            yield
            dve.wait_ge(root_ok, h + 1)
            fin.done(dve, dve.reciprocal(r, r))
            yield
            fin.done(dve, dve.tensor_tensor(tmp, r, r, ALU.mult))
            fin.done(dve, dve.tensor_tensor(tmp, tmp, ms, ALU.mult))
            yield
            fin.done(dve, dve.tensor_scalar(tmp, tmp, -0.5, 1.5, ALU.mult, ALU.add))
            fin.done(dve, dve.tensor_tensor(r, r, tmp, ALU.mult))
            yield
            dve.scalar_tensor_tensor(out=mixed[:, ds(h, 1), 0:NLAT].squeeze(1), in0=o, scalar=ngain[:, 0:1], in1=r,
                                     op0=ALU.mult, op1=ALU.mult).then_inc(o_used, 1)
            assert fin.n == fin.per
            fin.n = 0

        def head(h, par, first, last):
            beside = iter(()) if first else finish(h - 1)
            soft.loop(h, 5 * QT)

            def maxima(t):
                for m in range(2):
                    st = stat[t % 2][m]
                    dve.wait_ge(s_mm, 2 * QT * h + 2 * t + m + 1)
                    soft.done(dve, dve.tensor_reduce(st[:, 0:1], ps[:, 2 * m:2 * m + 2, 0:384], AX.XY, ALU.max))
                    dve.tensor_scalar(st[:, 1:2], st[:, 0:1], -HD ** -0.5, None, ALU.mult).then_inc(max_ok, 1)

            maxima(0)
            next(beside, None)
            for t in range(QT):
                s0, s1 = stat[t % 2]
                dve.wait_ge(exp_ok, 2 * QT * h + 2 * t + 2)
                soft.inc(dve.reciprocal(s0[:, 3:4], s0[:, 2:3]))
                soft.done(dve, dve.reciprocal(s1[:, 3:4], s1[:, 2:3]))
                soft.done(dve, dve.tensor_scalar(p[t % 2][1], p[t % 2][1], s1[:, 3:4], lam[:, 4:5], ALU.mult, ALU.mult))
                dve.scalar_tensor_tensor(out=p[t % 2][0], in0=p[t % 2][0], scalar=s0[:, 3:4], in1=p[t % 2][1],
                                         op0=ALU.mult, op1=ALU.add).then_inc(p_ok, 1)
                if t + 1 < QT:
                    maxima(t + 1)
                if not last:
                    for u in FIRST_HALF[t] + SECOND_HALF[t]:
                        unit(h + 1, 1 - par, u)
                next(beside, None)
            assert soft.n == soft.per
            soft.n = 0

        dve.wait_ge(const_in, 5 * 16)
        for n in range(2):
            at = 2 * n * HD
            lam_steps.done(dve, dve.tensor_tensor(tmp[:, 0:HD], lam_in[:, at:at + HD], lam_in[:, at + HD:at + 2 * HD], ALU.mult))
            lam_steps.done(dve, dve.tensor_reduce(lam[:, n:n + 1], tmp[:, 0:HD], AX.X, ALU.add))
        dve.sem_inc(lam_a, 1)
        dve.wait_ge(lam_b, 1)
        lam_steps.done(dve, dve.tensor_tensor(lam[:, 4:5], lam[:, 3:4], lam[:, 2:3], ALU.subtract))
        lam_steps.done(dve, dve.tensor_scalar(lam[:, 4:5], lam[:, 4:5], -LAMBDA_INIT, None, ALU.add))
        lam_steps.done(dve, dve.tensor_scalar(ngain, ngain, 1.0 - LAMBDA_INIT, None, ALU.mult))
        prologue(unit)
        heads(dve, head)
        for _ in finish(H - 1):
            pass

    return {"sync": sync, "tensor": tensor, "scalar": scalar, "vector": vector}



def best_of(B, tiles):
    flat = B.x.rearrange("p c t -> p (c t)")
    n = tiles * 2 * HEADS * TOPK
    return [flat[:, s * n:s * n + n].rearrange("p (n h z k) -> p n h z k", n=tiles, h=HEADS, z=2) for s in range(2)]


def product_keys(B, layer, segs):
    t0, n_tok = segs[0][0], sum(seg[1] for seg in segs)
    tiles = n_tok // P
    top, top_i = best_of(B, tiles)
    ar, parts = Arena(B.peer_arena), Arena(B.part_arena)
    w_raw = [ar.take(C * P) for _ in range(2)]
    w = [parts.take(2 * C * P).rearrange("p (s c n) -> p s c n", s=2, c=C) for _ in range(2)]
    keys = ar.take(2 * P).rearrange("p (z k) -> p z k", z=2)
    q = [ar.take(T) for _ in range(2)]
    rest = ar.take(tiles * P).rearrange("p (n k) -> p n k", n=tiles)
    found = ar.take(tiles * TOPK).rearrange("p (n k) -> p n k", n=tiles)
    found_i = ar.take(tiles * TOPK, U32).rearrange("p (n k) -> p n k", n=tiles)
    w_in = [B.sem(f"keys_wq_in{s}") for s in range(2)]
    names = ("keys_in", "w_high", "w_split", "q_mm", "q_ev", "s_mm", "s_ev", "chain", "passed")
    const_in, w_high, w_split, q_mm, q_ev, s_mm, s_ev, chain_s, passed = (B.sem(f"keys_{x}") for x in names)
    ps = B.ps
    PASSES = ((0, 0), (0, 1), (1, 0))
    Q_BANK = (0, 6)

    def settle(dve):
        dve.sem_inc(passed, 1)

    def sync(sp):
        sp.dma_start(keys, B.a["subkeys"][layer]).then_inc(const_in, 16)
        with sp.Fori(0, HEADS) as i:
            for z in range(2):
                sp.wait_ge(w_split, 2 * i + z + 1)
                sp.dma_start(w_raw[z], B.a["peer_wq"][layer, ds(2 * i + z, 1)].squeeze(0).rearrange(
                    "p c n -> p (c n)")).then_inc(w_in[z], 16)

    def tensor(pe):
        def project(j, z):
            pe.wait_ge(w_split, j + 3)
            pe.wait_ge(q_ev, j + 1)
            for (s0, m, which) in segs:
                todo = [(c, a, b) for c in range(C) for a, b in PASSES]
                for at, (c, a, b) in enumerate(todo):
                    mm = pe.matmul(ps[:, Q_BANK[z] + which, 0:m], w[z][:, a, c, :], B.xr[:, b, c, s0:s0 + m],
                                   start=at == 0, stop=at == len(todo) - 1)
            mm.then_inc(q_mm, 1)

        def score(j, z):
            pe.wait_ge(q_ev, j + 3)
            pe.wait_ge(s_ev, j + 1)
            for t in range(tiles):
                mm = pe.matmul(ps[:, 2 + 2 * z + t // 4, t % 4 * P:t % 4 * P + P],
                               q[z][:, t * P:t * P + P], keys[:, z, :], start=True, stop=True)
            mm.then_inc(s_mm, 1)

        pe.sem_inc(q_mm, 2)
        pe.wait_ge(const_in, 16)
        project(0, 0)
        with pe.Fori(0, HEADS - 1) as i:
            project(2 * i + 1, 1)
            score(2 * i, 0)
            project(2 * i + 2, 0)
            score(2 * i + 1, 1)
        project(2 * HEADS - 1, 1)
        score(2 * HEADS - 2, 0)
        score(2 * HEADS - 1, 1)

    def scalar(act):
        act.sem_inc(q_ev, 2)

        def split_w(j, z):
            act.wait_ge(w_in[z], 8 * j - 8 * z + 16)
            act.wait_ge(q_mm, j + 1)
            act.copy(w[z][:, 0].rearrange("p c n -> p (c n)"), w_raw[z]).then_inc(w_high, 1)

        def take(j, z):
            act.wait_ge(s_ev, j + 1)
            act.wait_ge(q_mm, j + 3)
            for (s0, m, which) in segs:
                ins = act.copy(q[z][:, s0 - t0:s0 - t0 + m], ps[:, Q_BANK[z] + which, 0:m])
            ins.then_inc(q_ev, 1)

        split_w(0, 0)
        split_w(1, 1)
        with act.Fori(0, HEADS - 1) as i:
            for z in range(2):
                take(2 * i + z, z)
                split_w(2 * i + z + 2, z)
        for z in range(2):
            take(2 * HEADS - 2 + z, z)

    def gpsimd(pool):
        pool.sem_inc(w_split, 2)
        with pool.Fori(0, HEADS) as i:
            for z in range(2):
                pool.wait_ge(w_high, 2 * i + z + 1)
                pool.tensor_tensor(w[z][:, 1].rearrange("p c n -> p (c n)"), w_raw[z],
                                   w[z][:, 0].rearrange("p c n -> p (c n)").bitcast(F32), ALU.subtract).then_inc(w_split, 1)

    def vector(dve):
        chain = Chain(chain_s)
        dve.sem_inc(s_ev, 2)
        with dve.Fori(0, HEADS) as i:
            chain.loop(i, 2 * (5 * tiles + 2))
            for z in range(2):
                dve.wait_ge(s_mm, 2 * i + z + 1)
                scores = [ps[:, 2 + 2 * z + t // 4, t % 4 * P:t % 4 * P + P] for t in range(tiles)]
                first = [found[:, t, 0:8] for t in range(tiles)]
                last = [found[:, t, 8:16] for t in range(tiles)]
                settle(dve)
                for t in range(tiles):
                    chain.inc(dve.max(first[t], scores[t]))
                chain.wait(dve)
                settle(dve)
                for t in range(tiles):
                    chain.inc(dve.max_index(found_i[:, t, 0:8], first[t], scores[t]))
                    chain.inc(dve.match_replace(rest[:, t, :], first[t], scores[t], LOWEST))
                chain.wait(dve)
                dve.sem_inc(s_ev, 1)
                for t in range(tiles):
                    chain.inc(dve.max(last[t], rest[:, t, :]))
                chain.wait(dve)
                settle(dve)
                for t in range(tiles):
                    chain.inc(dve.max_index(found_i[:, t, 8:16], last[t], rest[:, t, :]))
                chain.wait(dve)
                chain.inc(dve.tensor_scalar(top[:, :, ds(i, 1), z, :].squeeze(2), found, 0.0, None, ALU.add))
                chain.inc(dve.tensor_scalar(top_i[:, :, ds(i, 1), z, :].squeeze(2), found_i, 0.0, None, ALU.add))
                chain.wait(dve)
        chain.end(HEADS)

    return {"sync": sync, "tensor": tensor, "scalar": scalar, "gpsimd": gpsimd, "vector": vector}


def gates(B, layer, segs):
    t0, n_tok = segs[0][0], sum(seg[1] for seg in segs)
    tiles = n_tok // P
    top, top_i = best_of(B, tiles)
    ar = Arena(B.gate_arena)
    LOT = 2 * QUAD
    LOT_ACT = 4
    out = [ar.take(KEYS * TG).rearrange("p (j t) -> p j t", j=KEYS) for _ in range(2)]
    row, eq_j, col = ([ar.take(LOT * P).rearrange("p (t k) -> p t k", t=LOT) for _ in range(2)] for _ in range(3))
    cand = [ar.take(HEADS * 256).rearrange("p (h k) -> p h k", h=HEADS) for _ in range(2)]
    eq = [x.rearrange("p h (k a) -> p h k a", a=TOPK) for x in cand]
    ar_x = Arena(B.x.rearrange("p c t -> p (c t)")[:, 4 * tiles * PAIRS:])
    best = ar_x.take(PAIRS).rearrange("p (h k) -> p h k", h=HEADS)
    best_j = ar_x.take(PAIRS, U32).rearrange("p (h k) -> p h k", h=HEADS)
    digit_u = [ar.take(PAIRS, U32) for _ in range(2)]
    digit = [ar_x.take(PAIRS) for _ in range(2)]
    chosen = [ar_x.take(PAIRS) for _ in range(3)]
    turned = ar_x.take(3 * P).rearrange("p (n t) -> p n t", n=3)
    total, inv = ar_x.take(HEADS), ar_x.take(HEADS)
    apart = ar_x.take(LOT_ACT * P).rearrange("p (t k) -> p t k", t=LOT_ACT)
    iota = ar_x.take(P)
    MOD = 6 * C // tiles
    mod = ModTiles(B, (ar, ar_x), "mod2", 6 * C, 1, B.ps[:, 6, 0:2 * MOD]) if layer == 0 else None
    gate = chosen[2].rearrange("p (h k) -> p h k", h=HEADS)
    LOTS = P // LOT
    EXP_AT = 9
    names = ("iota_in", "turn_mm", "turned_ok", "shifted", "exp_ok", "chosen_ok", "row_ok", "row_act_ok", "apart_ok", "eq_ok",
             "col_ok", "g_mm", "g_ev", "out0", "out1", "chain", "passed")
    (iota_in, turn_mm, turned_ok, shifted, exp_ok, chosen_ok, row_ok, row_act_ok, apart_ok, eq_ok,
     col_ok, g_mm, g_ev, out0, out1, chain_s, passed) = (B.sem(f"gates_{x}") for x in names)
    g_out = (out0, out1)
    ps = B.ps
    grid = [P, HEADS, TOPK, TOPK]

    def settle(dve):
        dve.sem_inc(passed, 1)

    def sync(sp):
        sp.dma_start(iota, B.a["iota"]).then_inc(iota_in, 16)
        with sp.Fori(0, tiles) as i:
            for s in range(2):
                for m in (range(MOD - 2), range(MOD - 2, MOD))[s] if mod else ():
                    mod.load(sp, MOD * i + m, m % 2)
                sp.wait_ge(g_ev, 2 * LOTS * i + LOTS * (s + 1) + 2)
                sp.dma_start(B.g_dram[ds(2 * i + s, 1)].squeeze(0), out[s].rearrange("p j t -> p (j t)")).then_inc(g_out[s], 16)
        for s in range(2):
            sp.wait_ge(g_out[s], 16 * tiles + 16)

    def tensor(pe):
        def turn(i):
            pe.wait_ge(chosen_ok, i + 1)
            for n in range(3):
                mm = pe.transpose(ps[:, 4, n * P:n * P + P], chosen[n], B.ident[:, :])
            mm.then_inc(turn_mm, 1)

        def lots(i):
            for g in range(LOTS):
                s = g % 2
                if mod and g == 1:
                    pe.wait_ge(mod.added, i + 1)
                if mod and s == 1:
                    mod.multiply(pe, MOD * i + g // 2, g // 2 % 2, g // 2)
                pe.wait_ge(row_ok, LOTS * i + g + 1)
                pe.wait_ge(row_act_ok, LOTS * i + g + 2)
                pe.wait_ge(col_ok, LOTS * i + g + 1)
                for half in range(2):
                    pe.wait_ge(g_ev, 2 * LOTS * i + 2 * g + half + 1)
                    for n in range(QUAD):
                        t = half * QUAD + n
                        mm = pe.matmul(ps[:, half, n * P:n * P + P], row[s][:, t, :], col[s][:, t, :], start=True, stop=True)
                    mm.then_inc(g_mm, 1)

        if mod:
            assert MOD == LOTS // 2
            pe.sem_inc(mod.used, 2)
        turn(0)
        with pe.Fori(0, tiles - 1) as i:
            lots(i)
            turn(i + 1)
        lots(tiles - 1)

    def scalar(act):
        def exp(i):
            act.wait_ge(shifted, i + 1)
            act.activation(chosen[2], chosen[2], ACT.Exp).then_inc(exp_ok, 1)

        def rows(i, g):
            s, some = g % 2, row[g % 2][:, 0:LOT_ACT]
            if g >= 2:
                act.wait_ge(g_mm, 2 * LOTS * i + 2 * g - 2)
            act.wait_ge(row_act_ok, LOTS * i + g + 1)
            for t in range(LOT_ACT):
                at = g * LOT + t
                ins = act.activation(apart[:, t, :], iota, ACT.Abs, scale=-1.0, bias=turned[:, 0, at:at + 1])
            ins.then_inc(apart_ok, 1)
            act.wait_ge(apart_ok, LOTS * i + g + 1)
            act.activation(some, apart, ACT.Relu, scale=-1.0, bias=1.0).then_inc(row_act_ok, 1)

        def take(i, g):
            for half in range(2):
                to, at = out[2 * g // LOTS], (2 * g + half) % LOTS * QUAD
                act.wait_ge(g_mm, 2 * LOTS * i + 2 * g + half + 1)
                act.copy(to[:, :, at:at + QUAD].rearrange("p j t -> p t j"),
                         ps[:, half, :].rearrange("p (t j) -> p t j", t=QUAD)).then_inc(g_ev, 1)

        def lots(i, last):
            act.wait_ge(turned_ok, i + 1)
            for g in range(LOTS + 1):
                if g < LOTS:
                    rows(i, g)
                if g:
                    if (g - 1) % (LOTS // 2) == 0:
                        act.wait_ge(g_out[2 * (g - 1) // LOTS], 16 * i + 16)
                    take(i, g - 1)
                if g == EXP_AT and not last:
                    exp(i + 1)

        act.sem_inc(g_ev, 2)
        act.sem_inc(row_act_ok, 1)
        act.sem_inc(out0, 16)
        act.sem_inc(out1, 16)
        act.wait_ge(iota_in, 16)
        exp(0)
        with act.Fori(0, tiles - 1) as i:
            lots(i, False)
        lots(tiles - 1, True)

    def gpsimd(pool):
        with pool.Fori(0, tiles) as i:
            for g in range(LOTS):
                s, at = g % 2, g * LOT
                if g >= 2:
                    pool.wait_ge(g_mm, 2 * LOTS * i + 2 * g - 2)
                pool.wait_ge(eq_ok, LOTS * i + g + 1)
                pool.tensor_tensor(col[s], eq_j[s], turned[:, 2, at:at + LOT].unsqueeze(2).to_broadcast([P, LOT, P]),
                                   ALU.mult).then_inc(col_ok, 1)

    def vector(dve):
        chain = Chain(chain_s)

        def choose(i):
            here, here_i = (x[:, ds(i, 1)].squeeze(1) for x in (top, top_i))
            chain.done(dve, dve.tensor_tensor(
                cand[0].rearrange("p h (a b) -> p h a b", a=TOPK), here[:, :, 0, :].unsqueeze(3).to_broadcast(grid),
                here[:, :, 1, :].unsqueeze(2).to_broadcast(grid), ALU.add))
            yield
            settle(dve)
            for h in range(HEADS):
                chain.inc(dve.max(best[:, h, 0:8], cand[0][:, h, :]))
            chain.wait(dve)
            yield
            settle(dve)
            for h in range(HEADS):
                chain.inc(dve.max_index(best_j[:, h, 0:8], best[:, h, 0:8], cand[0][:, h, :]))
                chain.inc(dve.match_replace(cand[1][:, h, :], best[:, h, 0:8], cand[0][:, h, :], LOWEST))
                if h == HEADS // 2:
                    yield
                    settle(dve)
            chain.wait(dve)
            yield
            settle(dve)
            for h in range(HEADS):
                chain.inc(dve.max(best[:, h, 8:16], cand[1][:, h, :]))
            chain.wait(dve)
            yield
            settle(dve)
            for h in range(HEADS):
                chain.inc(dve.max_index(best_j[:, h, 8:16], best[:, h, 8:16], cand[1][:, h, :]))
            chain.inc(dve.tensor_tensor(gate, best, best[:, :, 0:1].to_broadcast([P, HEADS, TOPK]), ALU.subtract))
            chain.wait(dve)
            dve.sem_inc(shifted, 1)
            yield
            jj = best_j.rearrange("p h k -> p (h k)")
            chain.inc(dve.tensor_scalar(digit_u[0], jj, 4, None, ALU.logical_shift_right))
            chain.inc(dve.tensor_scalar(digit_u[1], jj, TOPK - 1, None, ALU.bitwise_and))
            chain.wait(dve)
            for z in range(2):
                chain.inc(dve.tensor_copy(digit[z], digit_u[z]))
            chain.wait(dve)
            for z in range(2):
                chain.inc(dve.tensor_tensor(
                    eq[z].rearrange("p h k a -> p (h k) a"), digit[z].unsqueeze(2).to_broadcast([P, PAIRS, TOPK]),
                    iota[:, 0:TOPK].unsqueeze(1).to_broadcast([P, PAIRS, TOPK]), ALU.is_equal))
                yield
            chain.wait(dve)
            for z in range(2):
                chain.inc(dve.tensor_tensor(eq[z], eq[z], here_i[:, :, z, :].unsqueeze(2).to_broadcast(grid), ALU.mult))
                yield
            chain.wait(dve)
            for z in range(2):
                chain.inc(dve.tensor_reduce(chosen[z], eq[z].rearrange("p h k a -> p (h k) a"), AX.X, ALU.add))
                yield
            dve.wait_ge(exp_ok, i + 1)
            chain.done(dve, dve.tensor_reduce(total, gate, AX.X, ALU.add))
            chain.done(dve, dve.reciprocal(inv, total))
            chain.done(dve, dve.tensor_tensor(gate, gate, inv.unsqueeze(2).to_broadcast([P, HEADS, TOPK]), ALU.mult))
            dve.sem_inc(chosen_ok, 1)

        def turn(i):
            dve.wait_ge(turn_mm, i + 1)
            dve.tensor_copy(turned, ps[:, 4, 0:3 * P].rearrange("p (n t) -> p n t", n=3)).then_inc(turned_ok, 1)

        def lots(i, beside):
            for g in range(LOTS):
                s = g % 2
                if g >= 2:
                    dve.wait_ge(col_ok, LOTS * i + g - 1)
                    dve.wait_ge(g_mm, 2 * LOTS * i + 2 * g - 2)
                dve.wait_ge(turned_ok, i + 1)
                for n, t, to, sem in ((1, 0, eq_j[s], eq_ok), (0, LOT_ACT, row[s][:, LOT_ACT:], row_ok)):
                    dve.tensor_tensor(to, iota.unsqueeze(1).to_broadcast([P, LOT - t, P]),
                                      turned[:, n, g * LOT + t:g * LOT + LOT].unsqueeze(2).to_broadcast([P, LOT - t, P]),
                                      ALU.is_equal).then_inc(sem, 1)
                next(beside, None)
            for _ in beside:
                pass
            dve.wait_ge(g_mm, 2 * LOTS * i + 2 * LOTS)
            if mod:
                dve.wait_ge(mod.used, MOD * i + MOD + 2)
                mod.add(dve, i, MOD)

        if mod:
            dve.sem_inc(mod.added, 1)
        dve.wait_ge(iota_in, 16)
        for _ in choose(0):
            pass
        turn(0)
        chain.base, chain.n = chain.n, 0
        with dve.Fori(0, tiles - 1) as i:
            chain.loop(i, 55)
            lots(i, choose(i + 1))
            turn(i + 1)
        chain.end(tiles - 1)
        lots(tiles - 1, iter(()))

    return {"sync": sync, "tensor": tensor, "scalar": scalar, "gpsimd": gpsimd, "vector": vector}


def experts(B, layer, segs):
    t0, n_tok = segs[0][0], sum(seg[1] for seg in segs)
    NG = n_tok // TG
    PAIRN = KEYS // 2
    PASSES = ((0, 0), (0, 1), (1, 0))
    acc = B.x
    ar, parts = Arena(B.peer_arena), Arena(B.part_arena)
    u_raw = [ar.take(C * P) for _ in range(2)]
    v_raw = [ar.take(D) for _ in range(2)]
    g = [ar.take(NG * 2 * TG).rearrange("p (n j t) -> p n j t", n=NG, j=2) for _ in range(2)]
    gelu = [ar.take(n_tok) for _ in range(2)]
    wt = [ar.take(n_tok) for _ in range(2)]
    u = [parts.take(2 * C * P).rearrange("p (s c n) -> p s c n", s=2, c=C) for _ in range(2)]
    v = [parts.take(2 * D).rearrange("p (s d) -> p s d", s=2) for _ in range(2)]
    w = [parts.take(2 * n_tok).rearrange("p (s t) -> p s t", s=2) for _ in range(4)]
    u_in, v_in, g_in = ([B.sem(f"exp_{x}{s}") for s in range(2)] for x in ("u_in", "v_in", "g_in"))
    names = ("u_high", "u_split", "v_high", "v_split", "s_mm", "gelu_ok", "wt_ok", "w_high", "w_split", "y_mm", "y_ev")
    u_high, u_split, v_high, v_split, s_mm, gelu_ok, wt_ok, w_high, w_split, y_mm, y_ev = (
        B.sem(f"exp_{x}") for x in names)
    ps = B.ps
    v_dram = B.a["peer_v"][layer].rearrange("(i j) d -> i j d", j=KEYS)

    def pairs(engine, body):
        body(0, 0, True, False)
        with engine.Fori(0, PAIRN // 2 - 1) as i:
            body(2 * i + 1, 1, False, False)
            body(2 * i + 2, 0, False, False)
        body(PAIRN - 1, 1, False, True)

    def sync(sp):
        def load_v(n):
            for k in range(2):
                sp.wait_ge(v_split, 2 * n + k + 1)
                sp.dma_start(v_raw[k], v_dram[:, ds(2 * n + k, 1), :].squeeze(1)).then_inc(v_in[k], 16)

        def body(n, parity, first, last):
            for k in range(2):
                sp.wait_ge(u_split, 2 * n + k + 1)
                sp.dma_start(u_raw[k], B.a["peer_u"][layer, ds(2 * n + k, 1)].squeeze(0).rearrange(
                    "p c n -> p (c n)")).then_inc(u_in[k], 16)
            sp.wait_ge(wt_ok, 2 * n + 2)
            sp.dma_start(g[parity], B.g_dram[0:NG, :, ds(n * 2 * TG, 2 * TG)].rearrange("n i k -> i n k")).then_inc(
                g_in[parity], 16)
            if not first:
                load_v(n - 1)
            if last:
                load_v(n)

        pairs(sp, body)

    def tensor(pe):
        pe.sem_inc(s_mm, 2)
        pe.sem_inc(y_mm, C)

        def values(n, parity):
            pe.wait_ge(v_split, 2 * n + 4)
            pe.wait_ge(w_split, 2 * n + 4 + 2)
            for c in range(C):
                pe.wait_ge(y_ev, n * C + c + 1)
                for (s0, m, which) in segs:
                    todo = [(k, a, b) for k in range(2) for a, b in PASSES]
                    for at, (k, a, b) in enumerate(todo):
                        mm = pe.matmul(ps[:, 4 + 2 * (c % 2) + which, 0:m], v[k][:, a, c * P:c * P + P],
                                       w[2 * parity + k][:, b, s0 - t0:s0 - t0 + m],
                                       start=at == 0, stop=at == len(todo) - 1)
                mm.then_inc(y_mm, 1)

        def body(n, parity, first, last):
            for k in range(2):
                pe.wait_ge(u_split, 2 * n + k + 3)
                pe.wait_ge(gelu_ok, 2 * n + k + 1)
                for (s0, m, which) in segs:
                    todo = [(c, a, b) for c in range(C) for a, b in PASSES]
                    for at, (c, a, b) in enumerate(todo):
                        mm = pe.matmul(ps[:, 2 * k + which, 0:m], u[k][:, a, c, :], B.xr[:, b, c, s0:s0 + m],
                                       start=at == 0, stop=at == len(todo) - 1)
                mm.then_inc(s_mm, 1)
            if not first:
                values(n - 1, 1 - parity)
            if last:
                values(n, parity)

        pairs(pe, body)

    def scalar(act):
        act.sem_inc(gelu_ok, 2)

        def split_u(j, k):
            act.wait_ge(u_in[k], 8 * j - 8 * k + 16)
            act.wait_ge(s_mm, j + 1)
            act.copy(u[k][:, 0].rearrange("p c n -> p (c n)"), u_raw[k]).then_inc(u_high, 1)

        def split_v(n):
            for k in range(2):
                act.wait_ge(v_in[k], 16 * n + 16)
                act.wait_ge(y_mm, C * n + C)
                act.copy(v[k][:, 0], v_raw[k]).then_inc(v_high, 1)

        def weigh(n, parity, k, first):
            act.wait_ge(s_mm, 2 * n + k + 3)
            act.wait_ge(wt_ok, 2 * n + k + 3)
            for (s0, m, which) in segs:
                ins = act.activation(gelu[k][:, s0 - t0:s0 - t0 + m], ps[:, 2 * k + which, 0:m], ACT.Gelu)
            ins.then_inc(gelu_ok, 1)
            act.wait_ge(wt_ok, 2 * n + k + 5)
            if not first:
                act.wait_ge(y_mm, C * n)
            act.copy(w[2 * parity + k][:, 0], wt[k]).then_inc(w_high, 1)

        def body(n, parity, first, last):
            if first:
                split_u(0, 0)
            split_u(2 * n + 1, 1)
            if not first:
                split_v(n - 1)
            weigh(n, parity, 0, first)
            if not last:
                split_u(2 * n + 2, 0)
            weigh(n, parity, 1, first)
            if last:
                split_v(n)

        pairs(act, body)

    def gpsimd(pool):
        pool.sem_inc(v_split, 2)
        def split_v(n):
            for k in range(2):
                pool.wait_ge(v_high, 2 * n + k + 1)
                pool.tensor_tensor(v[k][:, 1], v_raw[k], v[k][:, 0].bitcast(F32), ALU.subtract).then_inc(v_split, 1)

        def body(n, parity, first, last):
            if not first:
                split_v(n - 1)
            if last:
                split_v(n)

        pairs(pool, body)

    def vector(dve):
        dve.sem_inc(u_split, 2)
        dve.sem_inc(w_split, 4)
        dve.sem_inc(y_ev, 1)
        dve.memset(acc[:, :, t0:], 0.0).then_inc(y_ev, 1)
        dve.sem_inc(wt_ok, 4)
        dve.wait_ge(y_ev, 2)

        def split_u(j, k):
            dve.wait_ge(u_high, j + 1)
            dve.tensor_tensor(u[k][:, 1].rearrange("p c n -> p (c n)"), u_raw[k],
                              u[k][:, 0].rearrange("p c n -> p (c n)").bitcast(F32), ALU.subtract).then_inc(u_split, 1)

        def weigh(n, parity, k):
            if k == 0:
                dve.wait_ge(g_in[parity], 8 * n - 8 * parity + 16)
            dve.wait_ge(gelu_ok, 2 * n + k + 3)
            dve.wait_ge(w_split, 2 * n + k + 3)
            dve.tensor_tensor(wt[k].rearrange("p (n t) -> p n t", n=NG), gelu[k].rearrange("p (n t) -> p n t", n=NG),
                              g[parity][:, :, k, :], ALU.mult).then_inc(wt_ok, 1)

        def split_w(n, parity, k):
            dve.wait_ge(w_high, 2 * n + k + 1)
            dve.tensor_tensor(w[2 * parity + k][:, 1], wt[k], w[2 * parity + k][:, 0].bitcast(F32),
                              ALU.subtract).then_inc(w_split, 1)

        def collect(n, cs):
            for c in cs:
                dve.wait_ge(y_mm, C * n + c + 1 + C)
                if c == 0:
                    dve.wait_ge(y_ev, C * n + 2)
                for (s0, m, which) in segs:
                    ins = dve.tensor_tensor(acc[:, c, s0:s0 + m], ps[:, 4 + 2 * (c % 2) + which, 0:m],
                                            acc[:, c, s0:s0 + m], ALU.add)
                ins.then_inc(y_ev, 1)

        def body(n, parity, first, last):
            if first:
                split_u(0, 0)
            split_u(2 * n + 1, 1)
            weigh(n, parity, 0)
            split_w(n, parity, 0)
            if not last:
                split_u(2 * n + 2, 0)
            weigh(n, parity, 1)
            if not first:
                collect(n - 1, range(1))
            split_w(n, parity, 1)
            if not first:
                collect(n - 1, range(1, C))
            if last:
                collect(n, range(C))

        pairs(dve, body)
        dve.wait_ge(y_ev, PAIRN * C + 2)
        for c in range(C):
            for (s0, m, which) in segs:
                dve.scalar_tensor_tensor(out=B.h[:, c, s0:s0 + m], in0=acc[:, c, s0:s0 + m],
                                         scalar=B.mod[:, layer, 5, c, which:which + 1], in1=B.h[:, c, s0:s0 + m],
                                         op0=ALU.mult, op1=ALU.add)

    return {"sync": sync, "tensor": tensor, "scalar": scalar, "gpsimd": gpsimd, "vector": vector}



def columns(w):
    k, m = w.shape
    return np.ascontiguousarray(w.reshape(k // P, P, m // P, P).transpose(2, 1, 0, 3))


def rows(w):
    k, m = w.shape
    return w.reshape(k // P, P, m).transpose(1, 0, 2)


def layout(i):
    f = {n: np.asarray(x) for n, x in i.items()}
    a = {}
    a["hidden"] = rows(np.concatenate([f["ctx"][0], f["x"][0]], 0).T)
    a["cond"] = rows(np.stack([f["c_ctx"], f["c"][0]], 1))
    a["w_mod"] = np.concatenate([columns(f["w_mod"][l]) for l in range(DEPTH)], 0)
    a["b_mod"] = f["b_mod"].reshape(DEPTH * 6 * C, P).T
    gains = [f["norm1_g"][0], f["norm1_g"][1], f["norm2_g"][0], f["norm2_g"][1], f["final_g"]]
    a["gains"] = np.stack(gains).reshape(5 * C, P).T
    hk = GLA_HEADS * P
    w = f["gla_w_in"][0]
    q, k, v, g = w[:, :hk], w[:, hk:2 * hk], w[:, 2 * hk:2 * hk + D], w[:, 2 * hk + D:2 * hk + 2 * D]
    a["gla_w_qkg"] = np.stack([np.concatenate([rows(q[:, n * P:n * P + P]), rows(k[:, n * P:n * P + P]),
                                               rows(g[:, n * GLA_DV:(n + 1) * GLA_DV])], 2) for n in range(GLA_HEADS)])
    a["gla_w_v"] = np.stack([rows(v[:, n * GLA_DV:(n + 1) * GLA_DV]) for n in range(GLA_HEADS)])
    a["gla_w_lo"] = rows(w[:, 2 * hk + 2 * D:])
    walpha = np.zeros((2, 2, GLA_RANK, hk), np.float32)
    walpha[0, 0], walpha[1, 1] = f["gla_w_alpha"][0]
    a["gla_w_alpha"] = np.concatenate([walpha.transpose(0, 2, 1, 3).reshape(2 * GLA_RANK, 2, hk), f["gla_b_alpha"][0][None]], 0)
    a["gla_norm_g"] = f["gla_norm_g"][0].reshape(-1, P).T
    a["gla_w_out"] = columns(f["gla_w_out"][0])
    w = f["diff_w_in"][0]
    a["diff_w_in"] = np.stack([np.concatenate([rows(w[:, n * D + h * P:n * D + h * P + P]) for n in range(3)], 2)
                               for h in range(DIFF_HEADS)])
    a["diff_lambda"] = np.broadcast_to(f["diff_lambda"][0].reshape(1, -1), (P, 4 * HD))
    a["diff_norm_g"] = f["diff_norm_g"][0].reshape(P, 1)
    a["diff_w_out"] = columns(f["diff_w_out"][0])
    a["peer_wq"] = np.stack([columns(f["peer_wq"][l]) for l in range(DEPTH)])
    a["subkeys"] = f["peer_subkeys"].transpose(0, 3, 1, 2)
    a["peer_u"] = f["peer_u"].reshape(DEPTH, KEYS, KEYS, C, P).transpose(0, 2, 4, 3, 1)
    a["peer_v"] = f["peer_v"]
    a["ident"] = np.eye(P, dtype=np.float32)
    a["iota"] = np.broadcast_to(np.arange(P, dtype=np.float32), (P, P))
    a["ones_row"] = np.ones((1, T), np.float32)
    a["range_sums"], a["gla_masks"] = gla_range_sums(), gla_masks()
    a["cos"], a["sin"], a["swap"] = rope_tables()
    return {"in_" + n: np.ascontiguousarray(x) for n, x in a.items()}


def kernel(**inputs):
    import concourse.bacc as bacc
    from concourse.bass_utils import run_bass_kernel_spmd

    nc = bacc.Bacc("TRN2", target_bir_lowering=False, num_devices=1)
    arrays = layout(inputs)
    a = {n[3:]: nc.dram_tensor(n, x.shape, mybir.dt.from_np(x.dtype), kind="ExternalInput").ap() for n, x in arrays.items()}
    out = nc.dram_tensor("out", (P, C, NLAT), F32, kind="ExternalOutput").ap()
    build(nc, a, out)
    r = run_bass_kernel_spmd(nc, [arrays], core_ids=[0])
    y = r.results[0]["out"]
    return np.ascontiguousarray(y.transpose(2, 1, 0)).reshape(1, NLAT, D)
```
